# Optimizing a Trainium2 kernel written in Bass

```python
import math
import jax, jax.numpy as jnp
from jax import lax
import numpy as np

D_MODEL = 1024
BATCH = 1
SEQ = 256
DEPTH = 2

MEM_LEN = 256
EPS = 1e-6
ROPE_BASE = 10000.0
RET_HEADS = 4
RET_DK = 128
RET_DV = 256
RET_CHUNK = 128
SWA_Q_HEADS = 16
SWA_KV_HEADS = 2
SWA_HD = 64
SWA_WINDOW = 128
MEM_HEADS = 4
MEM_HD = 256
D_FF = 2816
N_BRANCH = 3

RET_QK_W = RET_HEADS * RET_DK
RET_V_W = RET_HEADS * RET_DV
SWA_Q_W = SWA_Q_HEADS * SWA_HD
SWA_KV_W = SWA_KV_HEADS * SWA_HD
MEM_Q_W = MEM_HEADS * MEM_HD
SPLITS = [RET_QK_W, RET_QK_W, RET_V_W, RET_V_W, SWA_Q_W, SWA_KV_W, SWA_KV_W, MEM_Q_W, N_BRANCH * D_MODEL]
IN_W = sum(SPLITS)
SPLIT_POINTS = [sum(SPLITS[:i + 1]) for i in range(len(SPLITS) - 1)]
NEG_INF = -1e30

kernel_name = "hybrid_retention_swa_sink_memory_macaron"

def rmsnorm(x, g):
    xf = x.astype(jnp.float32)
    y = xf * lax.rsqrt(jnp.mean(xf * xf, axis=-1, keepdims=True) + EPS)
    return (y * g.astype(jnp.float32)).astype(x.dtype)

def swiglu(h, w1, w3, w2):
    return (jax.nn.silu(h @ w1) * (h @ w3)) @ w2

def rotary(x):
    S, d = x.shape[1], x.shape[-1]
    half = d // 2
    inv = ROPE_BASE ** (-jnp.arange(half, dtype=jnp.float32) / half)
    ang = jnp.arange(S, dtype=jnp.float32)[:, None] * inv[None, :]
    cos = jnp.cos(ang)[None, :, None, :]
    sin = jnp.sin(ang)[None, :, None, :]
    x1, x2 = x[..., :half], x[..., half:]
    return jnp.concatenate([x1 * cos - x2 * sin, x1 * sin + x2 * cos], axis=-1)

def retention(q, k, v):
    out_dtype = v.dtype
    B, S, H, dk = q.shape
    dv = v.shape[-1]
    C = RET_CHUNK
    N = S // C
    f32 = jnp.float32
    log_g = jnp.log1p(-jnp.power(2.0, -5.0 - jnp.arange(H, dtype=f32)))
    q = rotary(q.astype(f32))
    k = rotary(k.astype(f32)) * (dk ** -0.5)
    v = v.astype(f32)
    qc = q.reshape(B, N, C, H, dk)
    kc = k.reshape(B, N, C, H, dk)
    vc = v.reshape(B, N, C, H, dv)
    i = jnp.arange(C, dtype=f32)
    diff = i[:, None] - i[None, :]
    intra_decay = jnp.where(diff[None] >= 0,
                            jnp.exp(jnp.maximum(diff, 0.0)[None] * log_g[:, None, None]), 0.0)
    s = jnp.einsum('bnchd,bnshd->bnhcs', qc, kc) * intra_decay
    intra = jnp.einsum('bnhcs,bnshe->bnche', s, vc)
    zeta = jnp.exp((C - 1 - i)[:, None] * log_g[None, :])
    xi = jnp.exp((i + 1)[:, None] * log_g[None, :])
    chunk_state = jnp.einsum('bnchd,bnche->bnhde', kc * zeta[..., None], vc)
    g_chunk = jnp.exp(C * log_g)[:, None, None]

    def step(R, st):
        return R * g_chunk + st, R

    _, prev = lax.scan(step, jnp.zeros((B, H, dk, dv), f32), jnp.moveaxis(chunk_state, 1, 0))
    prev = jnp.moveaxis(prev, 0, 1)
    cross = jnp.einsum('bnchd,bnhde->bnche', qc * xi[..., None], prev)
    return (intra + cross).reshape(B, S, H, dv).astype(out_dtype)

def sliding_window_attention(q, k, v, sinks):
    B, S, Hq, hd = q.shape
    Hkv = k.shape[2]
    G = Hq // Hkv
    W = SWA_WINDOW
    N = S // W
    qb = q.reshape(B, N, W, Hkv, G, hd)
    kb = k.reshape(B, N, W, Hkv, hd)
    vb = v.reshape(B, N, W, Hkv, hd)
    pad = ((0, 0), (1, 0), (0, 0), (0, 0), (0, 0))
    kk = jnp.concatenate([jnp.pad(kb, pad)[:, :-1], kb], axis=2)
    vv = jnp.concatenate([jnp.pad(vb, pad)[:, :-1], vb], axis=2)
    s = jnp.einsum('bnqkgd,bnskd->bnkgqs', qb, kk,
                   preferred_element_type=jnp.float32) * (hd ** -0.5)
    qpos = jnp.arange(W)[:, None] + W
    kpos = jnp.arange(2 * W)[None, :]
    rel = qpos - kpos
    band = (rel >= 0) & (rel < W)
    first = (jnp.arange(N) == 0)[:, None, None] & (kpos < W)[None]
    valid = band[None] & ~first
    s = jnp.where(valid[None, :, None, None], s, NEG_INF)
    sink = sinks.astype(jnp.float32).reshape(Hkv, G)[None, None, :, :, None, None]
    m = jnp.maximum(jnp.max(s, axis=-1, keepdims=True), sink)
    p = jnp.exp(s - m)
    p = p / (jnp.sum(p, axis=-1, keepdims=True) + jnp.exp(sink - m))
    o = jnp.einsum('bnkgqs,bnskd->bnqkgd', p.astype(v.dtype), vv)
    return o.reshape(B, S, Hq * hd)

def memory_attention(q, mk, mv):
    B, S, H, d = q.shape
    s = jnp.einsum('bshd,bmhd->bhsm', q, mk, preferred_element_type=jnp.float32) * (d ** -0.5)
    p = jax.nn.softmax(s, axis=-1)
    o = jnp.einsum('bhsm,bmhd->bshd', p.astype(mv.dtype), mv)
    return o.reshape(B, S, H * d)

def setup_inputs(seed: int = 0) -> dict:
    key = jax.random.key(seed)
    ks = jax.random.split(key, 24)
    L, D, F = DEPTH, D_MODEL, D_FF

    def w(k, shape, fan_in):
        return jax.random.normal(k, shape, jnp.float32) * (fan_in ** -0.5)

    def gain(k, shape):
        return 1.0 + 0.02 * jax.random.normal(k, shape, jnp.float32)

    return {
        "x": jax.random.normal(ks[0], (BATCH, SEQ, D), jnp.float32),
        "mem": jax.random.normal(ks[1], (BATCH, MEM_LEN, D), jnp.float32),
        "norm_ffn1": gain(ks[2], (L, D)),
        "ffn1_w1": w(ks[3], (L, D, F), D),
        "ffn1_w3": w(ks[4], (L, D, F), D),
        "ffn1_w2": w(ks[5], (L, F, D), F),
        "norm_mix": gain(ks[6], (L, D)),
        "w_in": w(ks[7], (L, D, IN_W), D),
        "ret_gn": gain(ks[8], (L, RET_V_W)),
        "swa_sinks": 0.5 * jax.random.normal(ks[9], (L, SWA_Q_HEADS), jnp.float32),
        "norm_mem": gain(ks[10], (L, D)),
        "w_mem_kv": w(ks[11], (L, D, 2 * MEM_Q_W), D),
        "w_up_ret": w(ks[12], (L, RET_V_W, D), RET_V_W),
        "w_up_swa": w(ks[13], (L, SWA_Q_W, D), SWA_Q_W),
        "w_up_mem": w(ks[14], (L, MEM_Q_W, D), MEM_Q_W),
        "w_o": w(ks[15], (L, D, D), D),
        "norm_ffn2": gain(ks[16], (L, D)),
        "ffn2_w1": w(ks[17], (L, D, F), D),
        "ffn2_w3": w(ks[18], (L, D, F), D),
        "ffn2_w2": w(ks[19], (L, F, D), F),
        "norm_final": gain(ks[20], (D,)),
    }

def reference(x, mem, norm_ffn1, ffn1_w1, ffn1_w3, ffn1_w2, norm_mix, w_in, ret_gn, swa_sinks,
              norm_mem, w_mem_kv, w_up_ret, w_up_swa, w_up_mem, w_o, norm_ffn2, ffn2_w1,
              ffn2_w3, ffn2_w2, norm_final):
    B, S, D = x.shape
    for l in range(DEPTH):
        h = rmsnorm(x, norm_ffn1[l])
        x = x + 0.5 * swiglu(h, ffn1_w1[l], ffn1_w3[l], ffn1_w2[l])

        h = rmsnorm(x, norm_mix[l])
        proj = h @ w_in[l]
        rq, rk, rv, rg, sq, sk, sv, mq, gl = jnp.split(proj, SPLIT_POINTS, axis=-1)

        ret = retention(rq.reshape(B, S, RET_HEADS, RET_DK),
                        rk.reshape(B, S, RET_HEADS, RET_DK),
                        rv.reshape(B, S, RET_HEADS, RET_DV))
        ret = rmsnorm(ret, ret_gn[l].reshape(RET_HEADS, RET_DV))
        ret = ret.reshape(B, S, RET_V_W) * jax.nn.silu(rg)

        swa = sliding_window_attention(sq.reshape(B, S, SWA_Q_HEADS, SWA_HD),
                                       sk.reshape(B, S, SWA_KV_HEADS, SWA_HD),
                                       sv.reshape(B, S, SWA_KV_HEADS, SWA_HD),
                                       swa_sinks[l])

        mkv = rmsnorm(mem, norm_mem[l]) @ w_mem_kv[l]
        mk, mv = jnp.split(mkv, 2, axis=-1)
        mo = memory_attention(mq.reshape(B, S, MEM_HEADS, MEM_HD),
                              mk.reshape(B, MEM_LEN, MEM_HEADS, MEM_HD),
                              mv.reshape(B, MEM_LEN, MEM_HEADS, MEM_HD))

        gates = jax.nn.sigmoid(gl.reshape(B, S, N_BRANCH, D))
        merged = (gates[:, :, 0] * (ret @ w_up_ret[l])
                  + gates[:, :, 1] * (swa @ w_up_swa[l])
                  + gates[:, :, 2] * (mo @ w_up_mem[l]))
        x = x + merged @ w_o[l]

        h = rmsnorm(x, norm_ffn2[l])
        x = x + 0.5 * swiglu(h, ffn2_w1[l], ffn2_w3[l], ffn2_w2[l])
    return rmsnorm(x, norm_final)


_drawn_inputs = setup_inputs


def setup_inputs(seed=0):
    import zlib

    import numpy as np

    out = dict(_drawn_inputs(seed))
    spreads = {}
    factors = {'norm_ffn1': 2.939,
     'norm_mix': 2.793,
     'ret_gn': 6.356,
     'swa_sinks': 18.412,
     'norm_mem': 8.0,
     'norm_ffn2': 5.133,
     'norm_final': 8.732}
    for name, (base, spread) in spreads.items():
        noise = np.random.default_rng([zlib.crc32(name.encode()), seed]).standard_normal(out[name].shape)
        drawn = base * np.exp(spread * noise) if base else spread * noise
        out[name] = __import__('jax').numpy.asarray(drawn.astype(out[name].dtype))
    for name, factor in factors.items():
        out[name] = (out[name] * factor).astype(out[name].dtype)
    return out
```

```python
from contextlib import ExitStack

import numpy as np

import concourse.bass as bass
from concourse import mybir

F32 = mybir.dt.float32
F32R = mybir.dt.float32r
BF16 = mybir.dt.bfloat16
ACT = mybir.ActivationFunctionType
ALU = mybir.AluOpType
AXX = mybir.AxisListType.X

P = 128
D = 1024
SEQ = 256
MEM = 256
DEPTH = 2
EPS = 1e-6
DFF = 2816
KT = D // P
TT = SEQ // P
BLK = 512
UB = 4
UW = UB * BLK
FC = 256
NCH = DFF // FC
RING = 3

RET_H, RET_DK, RET_DV = 4, 128, 256
SWA_H, SWA_KV, HD, WIN = 16, 2, 64, 128
GRP = 4
NGRP = SWA_H // GRP
MEM_H, MEM_HD = 4, 256

W_IN_AT = {"rq": 0, "rk": 512, "rv": 1024, "rg": 2048, "sq": 3072, "skv": 4096, "mq": 4352, "gl": 5376}
CHUNKS = ["mk0", "sq0", "sq1", "skv", "mk1", "mv0", "mv1", "rq0", "rk0", "rv0", "rv1", "rg0", "rg1",
          "gs0", "gs1", "us0", "us1", "mq0", "mq1", "gr0", "gr1", "ur0", "ur1", "gm0", "gm1", "um0",
          "um1", "wo0", "wo1"]
FFN_UNITS = 3 * NCH
MIX_UNITS = 2 * len(CHUNKS) - 1
NU = 2 * FFN_UNITS + MIX_UNITS
MIX_AT = FFN_UNITS
FFN2_AT = FFN_UNITS + MIX_UNITS
assert NU % RING == 0 and MIX_AT % RING == 0 and FFN2_AT % RING == 0

UNITS = [(c, u, u == (c != "skv")) for c in CHUNKS[:-2] for u in range(1 if c == "skv" else 2)]
UNITS += [(c, u, u == 1) for u in range(2) for c in CHUNKS[-2:]]

AFTER = {0: ["xt0"], 1: ["xt1"], 7: ["sqt"], 8: ["skt"], 9: ["s0"], 10: ["mkt"], 11: ["e0"], 12: ["s1"],
         13: ["pt0"], 14: ["pv0", "e1"], 15: ["s2"], 16: ["pt1"], 17: ["pv1", "e2"], 18: ["s3"],
         19: ["pt2"], 20: ["pv2", "e3"], 21: ["rqt", "rkt"], 22: ["pt3"], 23: ["pv3"], 24: ["rs"],
         26: ["st"], 27: ["ro"], 29: ["re"], 33: ["rt"],
         38: ["mqt"], 40: ["ms"], 41: ["me"], 43: ["mpt"], 45: ["mpv"], 47: ["mt"],
         51: ["mg0"], 53: ["mg1"]}
INSIDE = {56: ["yt0"]}
STEPS = []
for _i, _u in enumerate(UNITS):
    STEPS.append(("unit", _i, *_u, INSIDE.get(_i, [])))
    STEPS += [("step", s) for s in AFTER.get(_i, [])]

FFN_ENDS = [u in (1, FFN_UNITS - 1) or (1 < u and u % RING == 0) for u in range(FFN_UNITS)]
ENDS = FFN_ENDS + [last for *_, last in UNITS] + FFN_ENDS
USED = [ENDS[:u + 1].count(False) for u in range(NU)]
USED_TURN = 2

G_FFN1, G_MIX, G_MEM, G_RET, G_FFN2 = (KT * i for i in range(5))
G_SINK = 5 * KT
NG = G_SINK + SWA_H
DVE_STEPS = 21


class Banks:

    def __init__(self):
        self.uses, self.hi, self.at = [0] * 8, [0] * 8, {}

    def add(self, name, bank, n=1, split=False):
        self.at[name] = (bank, self.uses[bank], self.hi[bank])
        self.uses[bank] += n
        self.hi[bank] += n * split


def plan_banks():
    banks = Banks()

    def ffn(f):
        banks.add(f"up{f}", 4, NCH)
        banks.add(f"up{f}t1", 5, NCH)
        banks.add(f"gt{f}", 6, NCH, split=True)
        for h in range(2):
            for t in range(TT):
                banks.add(f"down{f}_{h}{t}", 2 * h + t)

    def xt(name, bank):
        for j in range(2):
            banks.add(f"{name}_{j}", bank + j, split=True)

    xt("x0", 6)
    xt("x1", 2)
    ffn(1)
    turn = [0]

    def take(name, n, split=False):
        for j in range(n):
            banks.add(f"{name}_{j}", 4 + turn[0] % 4, split=split)
            turn[0] += 1

    sizes = {"xt0": (2, True), "xt1": (2, True), "sqt": (4, False), "skt": (1, False), "mkt": (4, False),
             "st": (4, True), "rqt": (2, False), "rkt": (2, False), "rs": (4, False), "ro": (4, False),
             "rt": (4, True), "mqt": (4, False), "ms": (4, False), "mpt": (4, False), "mpv": (4, False),
             "mt": (4, True), "mg0": (2, True), "mg1": (2, True)}
    sizes |= {f"s{g}": (4, False) for g in range(NGRP)}
    sizes |= {f"pt{g}": (3, False) for g in range(NGRP)} | {f"pv{g}": (1, False) for g in range(NGRP)}
    for s in STEPS:
        if s[0] == "unit":
            _, _, chunk, u, _, inside = s
            if "yt0" in inside:
                xt("y0", 6)
            if u == 0:
                for t in range(TT):
                    banks.add(f"{chunk}t{t}", 2 * (CHUNKS.index(chunk) % 2) + t)
        elif s[1] in sizes:
            take(s[1], *sizes[s[1]])
    xt("y1", 6)
    ffn(2)
    return banks


def build(nc, x_in, mem_in, memt_in, stream, gains_in, gfin_in, rot_in, decay_in, mask_in, ident_in, out):
    banks = plan_banks()
    where, USES, HIS = banks.at, banks.uses, banks.hi

    ctx = ExitStack()
    with ctx:
        top = [nc.sbuf_base]

        def place(name, shape, dt=F32, at=None):
            size = int(np.prod(shape[1:])) * (2 if dt == BF16 else 4)
            if at is None:
                top[0] = -(-top[0] // 32) * 32
                at, top[0] = top[0], top[0] + size
            return nc.alloc_sbuf_tensor_at(name, shape, dt, offset=at), at

        def new(name, shape, dt=F32, at=None):
            return place(name, shape, dt, at)[0]

        x = new("x", [P, TT, D])
        hT_hi = new("hT_hi", [P, KT, SEQ], F32R)
        hT_lo = new("hT_lo", [P, KT, SEQ], F32R)
        raw = new("raw", [P, RING, UW])
        w_hi = new("w_hi", [P, RING, UW], F32R)
        w_lo = new("w_lo", [P, RING, UW], F32R)
        bT_hi = new("bT_hi", [P, KT, SEQ], F32R)
        bT_lo = new("bT_lo", [P, KT, SEQ], F32R)
        stA, a_at = place("stA", [P, TT, D])
        memT = new("memT", [P, KT, MEM], at=a_at)
        gfin = new("gfin", [P, D], at=a_at)
        stB, b_at = place("stB", [P, TT, D])
        mkT = new("mkT", [P, KT, MEM])
        mv = new("mv", [P, TT, D])
        rqT, q_at = place("rqT", [P, RET_H, SEQ])
        rkT, k_at = place("rkT", [P, RET_H, SEQ])
        rot_a = new("rot_a", [P, BLK], at=k_at)
        rot_b = new("rot_b", [P, BLK], at=k_at + 4 * BLK)
        mqT = new("mqT", [P, KT, SEQ], at=q_at)
        rv, v_at = place("rv", [P, TT, D])
        merged = new("merged", [P, TT, D], at=v_at)
        srg, s_at = place("srg", [P, TT, D])
        mpT = new("mpT", [P, MEM_H, TT, SEQ], at=s_at)
        sqT, sq_at = place("sqT", [P, KT, SEQ])
        gates = new("gates", [P, TT, D], at=sq_at)
        skT = new("skT", [P, SWA_KV, SEQ])
        sv = new("sv", [P, TT, P])
        prob, p_at = place("prob", [P, 2, GRP, 3 * WIN])
        mprob = new("mprob", [P, MEM_H, TT, MEM], at=p_at)
        sdec = new("sdec", [P, RET_H, 3 * P], at=p_at)
        act_s = new("act_s", [P, TT, FC], at=p_at)
        act_g = new("act_g", [P, TT, FC], at=p_at + 2048)
        gT_hi = new("gT_hi", [P, 2, SEQ], F32R, at=p_at + 4096)
        gT_lo = new("gT_lo", [P, 2, SEQ], F32R, at=p_at + 6144)
        junk = new("junk", [P, TT, D], BF16, at=p_at + 8192)
        pT, pt_at = place("pT", [P, 3 * GRP, P])
        skd = new("skd", [P, TT, SWA_KV, 2, HD], at=pt_at)
        rot = new("rot", [P, 2, TT, P])
        decay = new("decay", [P, RET_H, 2 * P])
        mask = new("mask", [P, 2 * WIN])
        ident = new("ident", [P, P])
        gains = new("gains", [P, DEPTH, NG])
        cur = new("cur", [P, NG])
        msq = new("msq", [P, TT])
        rstd = new("rstd", [P, TT])
        msq_mem = new("msq_mem", [P, TT])
        rstd_mem = new("rstd_mem", [P, TT])
        msq_r = new("msq_r", [P, 2 * RET_H])
        rstd_r = new("rstd_r", [P, 2 * RET_H])
        eps = new("eps", [P, 2 * RET_H])
        mhalf = new("mhalf", [P, 2 * RET_H])
        smax = new("smax", [P, 2, GRP, 2])
        snm = new("snm", [P, 2, GRP, 2])
        ssink = new("ssink", [P, 2, GRP, 2])
        sexp = new("sexp", [P, 2, GRP, 2])
        ssum = new("ssum", [P, 2, GRP, 2])
        mmax = new("mmax", [P, MEM_H, TT])
        mnm = new("mnm", [P, MEM_H, TT])
        msum = new("msum", [P, MEM_H, TT])
        assert top[0] <= nc.sbuf_usable_end, top

        ps = [ctx.enter_context(nc.psum_tensor(f"bank{b}", [P, BLK], F32)) for b in range(8)]

        def sem(name):
            return ctx.enter_context(nc.semaphore(name))

        raw_loaded = [sem(f"raw_loaded{s}") for s in range(RING)]
        hi_split, lo_split, unit_used = sem("hi_split"), sem("lo_split"), sem("unit_used")
        psum_full = [sem(f"psum_full{b}") for b in range(8)]
        psum_hi = [sem(f"psum_hi{b}") for b in range(8)]
        psum_free = [sem(f"psum_free{b}") for b in range(8)]
        x_loaded, consts_loaded, tables_loaded, mem_loaded, memt_loaded = map(
            sem, ["x_loaded", "consts_loaded", "tables_loaded", "mem_loaded", "memt_loaded"])
        layer_consts, memt_hi, memt_lo = map(sem, ["layer_consts", "memt_hi", "memt_lo"])
        msq_ready, rstd_ready, mem_msq_ready, rstd_mem_ready = map(sem, ["msq_ready", "rstd_ready", "mem_msq_ready", "rstd_mem_ready"])
        rotated, pool_step, dve_step, gates_used = map(sem, ["rotated", "pool_step", "dve_step", "gates_used"])
        swa_max, swa_exp, retsq_ready, retstd_ready, mem_max = map(
            sem, ["swa_max", "swa_exp", "retsq_ready", "retstd_ready", "mem_max"])
        silu_ready = [sem(f"silu_ready{t}") for t in range(TT)]
        gfin_loaded, final_ready, out_stored = map(sem, ["gfin_loaded", "final_ready", "out_stored"])

        def full(l, name, c=0):
            b, i, _ = where[name]
            return psum_full[b], l * USES[b] + c + (i + 1)

        def room(l, name, c=0):
            b, i, _ = where[name]
            return psum_free[b], l * USES[b] + c + (i + 1)

        def out_of(l, name, c=0):
            b, i, _ = where[name]
            return psum_free[b], l * USES[b] + c + (i + 2)

        def hi_out(l, name, c=0):
            b, _, j = where[name]
            return psum_hi[b], l * HIS[b] + c + (j + 1)

        def used(l, unit, c=0):
            if not ENDS[unit]:
                return unit_used, l * USED[-1] + c * USED_TURN + USED[unit]
            if unit < MIX_AT or unit >= FFN2_AT:
                f, at = (1, 0) if unit < MIX_AT else (2, FFN2_AT)
                if unit - at == FFN_UNITS - 1:
                    return full(l, f"down{f}_11")
                return full(l, f"up{f}t1", c + (unit - at) // RING)
            return full(l, UNITS[unit - MIX_AT][0] + "t1")

        def bank(name):
            return ps[where[name][0]]

        def free(name):
            return psum_free[where[name][0]]

        def fullsem(name):
            return psum_full[where[name][0]]

        def hisem(name):
            return psum_hi[where[name][0]]

        def x_of_layer_before(eng, l, b):
            eng.wait_ge(psum_free[b], l * USES[b] + 1)

        SPLIT_TO = {"rt": (G_RET, bT_hi, bT_lo), "st": (None, bT_hi, bT_lo), "mt": (None, bT_hi, bT_lo)}

        block = ctx.enter_context(nc.Block())

        @block.sync
        def _(sp):
            for s in range(RING):
                sp.dma_start(raw[:, s], stream[s]).then_inc(raw_loaded[s], 16)
            with sp.Fori(1, DEPTH * NU // RING) as i:
                for s in range(RING):
                    sp.wait_ge(lo_split, i * RING + (s + 1 - RING))
                    sp.dma_start(raw[:, s], stream[i * RING + s]).then_inc(raw_loaded[s], 16)
            sp.wait_ge(final_ready, TT)
            sp.dma_start(out.rearrange("(t p) d -> p t d", p=P), stB[:, :, :]).then_inc(out_stored, 16)
            sp.wait_ge(out_stored, 16)

        @block.gpsimd
        def _(pool):
            pool.memset(eps[:, :], EPS).then_inc(pool_step, 1)
            pool.memset(mhalf[:, :], -0.5).then_inc(pool_step, 1)
            pool.wait_ge(pool_step, 2)

            def inv_rms(dst, src, n, done, step):
                pool.tensor_tensor(dst[:, 0:n], src[:, 0:n], eps[:, 0:n], ALU.add).then_inc(pool_step, 1)
                pool.wait_ge(pool_step, step)
                pool.tensor_tensor(dst[:, 0:n], dst[:, 0:n], mhalf[:, 0:n], ALU.pow).then_inc(done, 1)

            PER = 5 + 4 * 3
            with pool.Fori(0, DEPTH) as l:
                def at(n):
                    return l * PER + (2 + n)

                pool.wait_ge(msq_ready, l * 3 * TT + TT)
                inv_rms(rstd, msq, TT, rstd_ready, at(1))
                pool.wait_ge(mem_msq_ready, l * TT + TT)
                inv_rms(rstd_mem, msq_mem, TT, rstd_mem_ready, at(2))
                pool.wait_ge(msq_ready, l * 3 * TT + 2 * TT)
                inv_rms(rstd, msq, TT, rstd_ready, at(3))
                pool.wait_ge(tables_loaded, 16 * 3)
                n = 3
                for qk, name in enumerate(("rq0", "rk0")):
                    for t in range(TT):
                        pool.wait_ge(*out_of(l, f"{name}t{t}"))
                        src = stB[:, t, qk * BLK:(qk + 1) * BLK].rearrange("p (h d) -> p h d", h=RET_H)
                        av = rot_a[:, :].rearrange("p (h d) -> p h d", h=RET_H)
                        bv = rot_b[:, :].rearrange("p (h d) -> p h d", h=RET_H)
                        half = RET_DK // 2
                        cos = rot[:, 0, t].unsqueeze(1).broadcast_to([P, RET_H, P])
                        if n > 3:
                            pool.wait_ge(rotated, l * 4 + (qk * TT + t))
                        pool.tensor_tensor(av, src, cos, ALU.mult).then_inc(pool_step, 1)
                        for lo, hi in ((0, half), (half, 0)):
                            sin = rot[:, 1, t, lo:lo + half].unsqueeze(1).broadcast_to([P, RET_H, half])
                            pool.tensor_tensor(bv[:, :, lo:lo + half], src[:, :, hi:hi + half], sin, ALU.mult)\
                                .then_inc(pool_step, 1)
                        n += 3
                        pool.wait_ge(pool_step, at(n))
                        pool.tensor_tensor(src, av, bv, ALU.add).then_inc(rotated, 1)
                pool.wait_ge(retsq_ready, l * 2 * RET_H + 2 * RET_H)
                inv_rms(rstd_r, msq_r, 2 * RET_H, retstd_ready, at(n + 1))
                pool.wait_ge(msq_ready, l * 3 * TT + 3 * TT)
                inv_rms(rstd, msq, TT, rstd_ready, at(n + 2))
                assert n + 2 == PER
            pool.wait_ge(msq_ready, DEPTH * 3 * TT + TT)
            inv_rms(rstd, msq, TT, rstd_ready, DEPTH * PER + 3)

        @block.tensor
        def _(pe):
            for b in range(8):
                pe.nop().then_inc(psum_free[b], 1)
            pe.wait_ge(consts_loaded, 16 * 2)
            pe.wait_ge(x_loaded, 16)

            def three_passes(dst, xh, xl, slot, cols, first, last):
                a, b = cols
                nc.tensor.matmul(dst, xl, w_hi[:, slot, a:b], start=first, stop=False)
                nc.tensor.matmul(dst, xh, w_hi[:, slot, a:b], start=False, stop=False)
                return nc.tensor.matmul(dst, xh, w_lo[:, slot, a:b], start=False, stop=last)

            def tokens(t):
                return slice(t * P, (t + 1) * P)

            def project(l, unit, names, hi, lo, half, c=0, uc=0, inside=None):
                pe.wait_ge(lo_split, l * NU + uc + (unit + 1))
                for t in range(TT):
                    if t == 1 and inside:
                        inside()
                    if half == 0:
                        pe.wait_ge(*room(l, names[t], c))
                    for j in range(UB):
                        k = UB * half + j
                        last = three_passes(bank(names[t])[:, :], hi[:, k, tokens(t)], lo[:, k, tokens(t)],
                                            unit % RING, (j * BLK, (j + 1) * BLK), k == 0, k == KT - 1)
                    if half == 1:
                        last.then_inc(fullsem(names[t]), 1)
                if half == 0:
                    last.then_inc(unit_used, 1)

            def project_kv(l, unit, names):
                pe.wait_ge(lo_split, l * NU + (unit + 1))
                for t in range(TT):
                    pe.wait_ge(*room(l, names[t]))
                    for k in range(KT):
                        last = three_passes(bank(names[t])[:, 0:256], hT_hi[:, k, tokens(t)], hT_lo[:, k, tokens(t)],
                                            unit % RING, (k * 256, (k + 1) * 256), k == 0, k == KT - 1)
                    last.then_inc(fullsem(names[t]), 1)

            def wait_out(l, names, then, c=0):
                last = {where[name][0]: name for name in names}
                for b, name in last.items():
                    if b not in {where[t][0] for t in then}:
                        pe.wait_ge(*out_of(l, name, c))

            def transpose_to(l, name, src, k0, tiles=TT, c=0):
                pe.wait_ge(*room(l, name, c))
                for j in range(2):
                    for t in range(tiles):
                        at = (j * tiles + t) * P
                        last = nc.tensor.transpose(bank(name)[:, at:at + P], src(t, k0 + j), ident[:, :])
                last.then_inc(fullsem(name), 1)

            def token_major(buf):
                return lambda t, k: buf[:, t, k * P:(k + 1) * P]

            def x_transposes(l, name, h):
                for j in range(2):
                    transpose_to(l, f"{name}_{j}", token_major(x), UB * h + 2 * j)

            def ffn(l, f, at):
                up = (f"up{f}", f"up{f}t1")

                def transpose_g(c):
                    pe.wait_ge(*out_of(l, up[0], c))
                    pe.wait_ge(*out_of(l, up[1], c))
                    transpose_to(l, f"gt{f}", token_major(act_g), 0, c=c)

                def down(c, uc, unit, first, last_chunk):
                    pe.wait_ge(lo_split, l * NU + uc + (unit + 1))
                    pe.wait_ge(*out_of(l, f"gt{f}", c))
                    for h in range(2):
                        for t in range(TT):
                            name = f"down{f}_{h}{t}"
                            if first:
                                pe.wait_ge(*room(l, name))
                            for j in range(2):
                                i = three_passes(bank(name)[:, :], gT_hi[:, j, tokens(t)], gT_lo[:, j, tokens(t)],
                                                 unit % RING, ((2 * h + j) * BLK, (2 * h + j + 1) * BLK),
                                                 first and j == 0, last_chunk and j == 1)
                            if last_chunk:
                                i.then_inc(fullsem(name), 1)
                    if not last_chunk:
                        i.then_inc(unit_used, 1)

                if f == 1:
                    for h in range(2):
                        for t in range(TT):
                            x_of_layer_before(pe, l, 2 * h + t)
                        x_transposes(l, f"x{h}", h)

                def second_half():
                    for t in range(TT):
                        pe.wait_ge(*out_of(l, f"wo1t{t}"))
                    x_transposes(l, "y1", 1)

                for h in range(2):
                    for j in range(2):
                        pe.wait_ge(*out_of(l, "xy"[f - 1] + f"{h}_{j}"))
                    project(l, at + h, up, hT_hi, hT_lo, h, inside=second_half if f == 2 and h == 0 else None)

                def turn(c, uc, first):
                    transpose_g(c)
                    project(l, at + 2, up, hT_hi, hT_lo, 0, c + 1, uc)
                    project(l, at + 3, up, hT_hi, hT_lo, 1, c + 1, uc)
                    down(c, uc, at + 4, first, False)

                turn(0, 0, True)
                with pe.Fori(1, NCH - 1) as c:
                    turn(c, c * 3, False)
                transpose_g(NCH - 1)
                down(NCH - 1, 0, at + FFN_UNITS - 1, False, True)

            with pe.Fori(0, DEPTH) as l:
                ffn(l, 1, 0)

                def grp_scores(g):
                    for j in range(4):
                        pe.wait_ge(*room(l, f"s{g}_{j}"))
                    for b in range(2):
                        n = WIN * (b + 1)
                        for i in range(2):
                            for odd in range(2):
                                head, name = GRP * g + 2 * i + odd, f"s{g}_{2 * b + odd}"
                                rows = slice(HD * odd, HD * (odd + 1))
                                last = nc.tensor.matmul(bank(name)[:, i * n:(i + 1) * n], sqT[rows, head // 2, tokens(b)],
                                                        skT[rows, head // (SWA_H // SWA_KV), 0:n], start=True, stop=True)
                                if i == 1:
                                    last.then_inc(fullsem(name), 1)

                def grp_transposes(g):
                    pe.wait_ge(swa_exp, l * NGRP + (g + 1))
                    for j in range(3):
                        name = f"pt{g}_{j}"
                        pe.wait_ge(*room(l, name))
                        for i in range(4):
                            head, col = (i, 0) if j == 0 else (2 * (j - 1) + i // 2, WIN * (1 + i % 2))
                            last = nc.tensor.transpose(bank(name)[:, i * P:(i + 1) * P],
                                                       prob[:, g % 2, head, col:col + P], ident[:, :])
                        last.then_inc(fullsem(name), 1)

                def grp_values(g):
                    kv = GRP * g // (SWA_H // SWA_KV)
                    name = f"pv{g}_0"
                    wait_out(l, [f"pt{g}_{j}" for j in range(3)], [name])
                    pe.wait_ge(*room(l, name))
                    for i in range(GRP):
                        v = [sv[:, t, kv * HD:(kv + 1) * HD] for t in range(TT)]
                        o = bank(name)[:, 2 * i * HD:2 * (i + 1) * HD]
                        nc.tensor.matmul(o[:, 0:HD], pT[:, i, :], v[0], start=True, stop=True)
                        for t in range(TT):
                            last = nc.tensor.matmul(o[:, HD:2 * HD], pT[:, GRP + 2 * i + t, :], v[t],
                                                    start=t == 0, stop=t == TT - 1)
                    last.then_inc(fullsem(name), 1)

                def step(s):
                    if s in ("xt0", "xt1"):
                        h = int(s[2])
                        for t in range(TT):
                            pe.wait_ge(*out_of(l, f"down1_{h}{t}"))
                        x_transposes(l, s, h)
                    elif s == "yt0":
                        for t in range(TT):
                            pe.wait_ge(*out_of(l, f"wo0t{t}"))
                        x_transposes(l, "y0", 0)
                    elif s == "sqt":
                        wait_out(l, [f"sq{h}t{t}" for h in range(2) for t in range(TT)], ["sqt_0"])
                        for j in range(4):
                            transpose_to(l, f"sqt_{j}", token_major(stB), 2 * j)
                    elif s == "skt":
                        wait_out(l, [f"skvt{t}" for t in range(TT)], ["skt_0"])
                        transpose_to(l, "skt_0", lambda t, g: skd[:, t, g].rearrange("p a b -> p (a b)"), 0)
                    elif s == "mkt":
                        wait_out(l, [f"mk{h}t{t}" for h in range(2) for t in range(TT)], ["mkt_0"])
                        for j in range(4):
                            transpose_to(l, f"mkt_{j}", token_major(stA), 2 * j)
                    elif s in ("s0", "s1", "s2", "s3"):
                        grp_scores(int(s[1]))
                    elif s[:2] == "pt":
                        grp_transposes(int(s[2]))
                    elif s in ("pv0", "pv1", "pv2", "pv3"):
                        grp_values(int(s[2]))
                    elif s == "st":
                        wait_out(l, [f"pv{g}_0" for g in range(NGRP)], ["st_0"])
                        for j in range(4):
                            transpose_to(l, f"st_{j}", token_major(stA), 2 * j)
                    elif s in ("rqt", "rkt"):
                        qk = int(s == "rkt")
                        pe.wait_ge(rotated, l * 4 + 2 * (qk + 1))
                        for j in range(2):
                            transpose_to(l, f"{s}_{j}", lambda t, h: stB[:, t, (RET_H * qk + h) * P:(RET_H * qk + h + 1) * P],
                                         2 * j)
                    elif s == "rs":
                        wait_out(l, [f"{a}_{j}" for a in ("rqt", "rkt") for j in range(2)], ["rs_0"])
                        for h in range(RET_H):
                            name = f"rs_{h}"
                            pe.wait_ge(*room(l, name))
                            nc.tensor.matmul(bank(name)[:, 0:2 * P], rkT[:, h, 0:P], rqT[:, h, :], start=True, stop=True)
                            nc.tensor.matmul(bank(name)[:, 2 * P:3 * P], rkT[:, h, P:2 * P], rqT[:, h, P:2 * P],
                                             start=True, stop=True).then_inc(fullsem(name), 1)
                    elif s == "ro":
                        for h in range(RET_H):
                            name = f"ro_{h}"
                            wait_out(l, [f"rs_{h}"], [name])
                            pe.wait_ge(*room(l, name))
                            v = [rv[:, t, h * RET_DV:(h + 1) * RET_DV] for t in range(TT)]
                            nc.tensor.matmul(bank(name)[:, 0:RET_DV], sdec[:, h, 0:P], v[0], start=True, stop=True)
                            nc.tensor.matmul(bank(name)[:, RET_DV:], sdec[:, h, P:2 * P], v[0], start=True, stop=False)
                            nc.tensor.matmul(bank(name)[:, RET_DV:], sdec[:, h, 2 * P:3 * P], v[1],
                                             start=False, stop=True).then_inc(fullsem(name), 1)
                    elif s == "rt":
                        wait_out(l, [f"ro_{h}" for h in range(RET_H)], ["rt_0"])
                        for j in range(4):
                            transpose_to(l, f"rt_{j}", token_major(stB), 2 * j)
                    elif s == "mqt":
                        wait_out(l, [f"mq{h}t{t}" for h in range(2) for t in range(TT)], ["mqt_0"])
                        for j in range(4):
                            transpose_to(l, f"mqt_{j}", token_major(stA), 2 * j)
                    elif s == "ms":
                        wait_out(l, [f"mqt_{j}" for j in range(4)], ["ms_0"])
                        for h in range(MEM_H):
                            name = f"ms_{h}"
                            pe.wait_ge(*room(l, name))
                            for t in range(TT):
                                for k in range(2):
                                    last = nc.tensor.matmul(bank(name)[:, t * MEM:(t + 1) * MEM],
                                                            mqT[:, 2 * h + k, tokens(t)], mkT[:, 2 * h + k, :],
                                                            start=k == 0, stop=k == 1)
                            last.then_inc(fullsem(name), 1)
                    elif s == "mpt":
                        for h in range(MEM_H):
                            name = f"mpt_{h}"
                            wait_out(l, [f"ms_{h}"], [name])
                            transpose_to(l, name, lambda t, m: mprob[:, h, t, m * P:(m + 1) * P], 0)
                    elif s == "mpv":
                        for h in range(MEM_H):
                            name = f"mpv_{h}"
                            wait_out(l, [f"mpt_{h}"], [name])
                            pe.wait_ge(*room(l, name))
                            for t in range(TT):
                                for m in range(2):
                                    last = nc.tensor.matmul(bank(name)[:, t * MEM_HD:(t + 1) * MEM_HD],
                                                            mpT[:, h, m, tokens(t)],
                                                            mv[:, m, h * MEM_HD:(h + 1) * MEM_HD],
                                                            start=m == 0, stop=m == 1)
                            last.then_inc(fullsem(name), 1)
                    elif s == "mt":
                        wait_out(l, [f"mpv_{h}" for h in range(MEM_H)], ["mt_0"])
                        for j in range(4):
                            transpose_to(l, f"mt_{j}", token_major(stB), 2 * j)
                    elif s in ("mg0", "mg1"):
                        h = int(s[2])
                        pe.wait_ge(gates_used, l * 8 + (4 + TT * (h + 1)))
                        for j in range(2):
                            transpose_to(l, f"{s}_{j}", token_major(merged), UB * h + 2 * j)

                for s in STEPS:
                    if s[0] == "step":
                        step(s[1])
                        continue
                    _, i, chunk, half, _, inside = s
                    names = [f"{chunk}t{t}" for t in range(TT)]
                    if chunk == "skv":
                        project_kv(l, MIX_AT + i, names)
                        continue
                    hi, lo = (bT_hi, bT_lo) if chunk[0] == "u" or chunk[:2] in ("mk", "mv") else (hT_hi, hT_lo)
                    if chunk == "mk0" and half == 0:
                        pe.wait_ge(memt_lo, l + 1)
                    need = {("sq0", 0): ["xt0"], ("sq0", 1): ["xt1"], ("wo0", 0): ["mg0"], ("wo0", 1): ["mg1"]}
                    for name in need.get((chunk, half), []):
                        for j in range(2):
                            pe.wait_ge(*out_of(l, f"{name}_{j}"))
                    need = {"us0": "st", "ur0": "rt", "um0": "mt"}
                    if chunk in need:
                        for j in range(2 * half, 2 * half + 2):
                            pe.wait_ge(*out_of(l, f"{need[chunk]}_{j}"))
                    project(l, MIX_AT + i, names, hi, lo, half, inside=(lambda: [step(n) for n in inside]) if inside else None)
                ffn(l, 2, FFN2_AT)

        @block.scalar
        def _(act):
            for dst, src in ((gains, gains_in), (ident, ident_in)):
                act.dma_start(dst[:], src).then_inc(consts_loaded, 16)
            act.dma_start(x[:, :, :], x_in.rearrange("(t p) d -> p t d", p=P)).then_inc(x_loaded, 16)
            for dst, src in ((rot, rot_in), (decay, decay_in), (mask, mask_in)):
                act.dma_start(dst[:], src).then_inc(tables_loaded, 16)

            def squares(src, dst, done):
                for t in range(TT):
                    nc.scalar.activation(junk[:, t, :], src[:, t, :], ACT.Square, scale=D ** -0.5, accum_out=dst[:, t:t + 1]).then_inc(done, 1)

            def split(l, unit, uc=0):
                s = unit % RING
                act.wait_ge(raw_loaded[s], l * (NU // RING * 16) + uc * 16 + (unit // RING + 1) * 16)
                before = unit - RING
                if before >= 0:
                    act.wait_ge(*used(l, before, uc))
                nc.scalar.activation(w_hi[:, s], raw[:, s], ACT.Copy).then_inc(hi_split, 1)

            def split_on(l, f, unit):
                if f == 1:
                    split(l, unit)
                else:
                    with act.If(l < DEPTH - 1):
                        split(l, unit)

            def hi_parts(l, name, dst, k0, gain, c=0):
                act.wait_ge(*full(l, name, c))
                if gain is None:
                    nc.scalar.activation(dst[:, k0:k0 + 2, :].rearrange("p k t -> p (k t)"), bank(name)[:, :],
                                         ACT.Copy).then_inc(hisem(name), 1)
                    return
                for j in range(2):
                    k = k0 + j
                    i = nc.scalar.activation(dst[:, k, :], bank(name)[:, j * SEQ:(j + 1) * SEQ], ACT.Copy,
                                             scale=cur[:, gain + k:gain + k + 1])
                i.then_inc(hisem(name), 1)

            def ffn(l, f, at, gain):
                if f == 1:
                    for j in range(2):
                        hi_parts(l, f"x0_{j}", hT_hi, 2 * j, gain)
                    split(l, RING - 1)
                for j in range(2):
                    hi_parts(l, "xy"[f - 1] + f"1_{j}", hT_hi, UB + 2 * j, gain)
                act_x_squares(l, 0 if f == 1 else 2)
                split(l, at + 3)
                act.wait_ge(rstd_ready, l * 3 + (1 if f == 1 else 3))

                def silu(c):
                    for t in range(TT):
                        up = f"up{f}" + ("" if t == 0 else "t1")
                        act.wait_ge(*full(l, up, c))
                        nc.scalar.activation(act_s[:, t, :], bank(up)[:, 0:FC], ACT.Silu,
                                             scale=rstd[:, t:t + 1]).then_inc(silu_ready[t], 1)

                silu(0)
                split(l, at + 4)
                if f == 1:
                    act.wait_ge(memt_loaded, l * 16 + 16)
                    for k in range(KT):
                        i = nc.scalar.activation(bT_hi[:, k, :], memT[:, k, :], ACT.Copy,
                                                 scale=cur[:, G_MEM + k:G_MEM + k + 1])
                    i.then_inc(memt_hi, 1)
                    act.wait_ge(mem_loaded, l * 16 + 16)
                    squares(stB, msq_mem, mem_msq_ready)

                with act.Fori(0, NCH - 2) as c:
                    hi_parts(l, f"gt{f}", gT_hi, 0, None, c)
                    split(l, at + 5, c)
                    silu(c + 1)
                    split(l, at + 6, c)
                    split(l, at + 7, c)
                c = NCH - 2
                hi_parts(l, f"gt{f}", gT_hi, 0, None, c)
                split(l, at + 5 + 3 * c)
                silu(c + 1)
                split_on(l, f, at + 6 + 3 * c)
                hi_parts(l, f"gt{f}", gT_hi, 0, None, c + 1)
                split_on(l, f, at + 7 + 3 * c)
                if f == 1:
                    split(l, at + 8 + 3 * c)

            def act_x_squares(l, which):
                if which == 0:
                    for b in range(4):
                        x_of_layer_before(act, l, b)
                for h in range(2):
                    for t in range(TT):
                        if which:
                            act.wait_ge(*out_of(l, f"down1_{h}{t}" if which == 1 else f"wo{h}t{t}"))
                squares(x, msq, msq_ready)

            act.wait_ge(x_loaded, 16)
            for u in range(RING - 1):
                split(0, u)

            with act.Fori(0, DEPTH) as l:
                act.wait_ge(layer_consts, l + 1)
                act.dma_start(memT[:, :, :], memt_in).then_inc(memt_loaded, 16)
                act.dma_start(stB[:, :, :], mem_in.rearrange("(t p) d -> p t d", p=P)).then_inc(mem_loaded, 16)
                ffn(l, 1, 0, G_FFN1)

                def scaled(dst, chunk, t, scale, func=ACT.Copy, cols=(0, BLK)):
                    name = f"{chunk}t{t}"
                    return nc.scalar.activation(dst, bank(name)[:, cols[0]:cols[1]], func, scale=scale[:, t:t + 1])

                def evacuate(chunk):
                    kind, half = chunk[:2], int(chunk[2]) if chunk != "skv" else 0
                    cols = slice(half * BLK, (half + 1) * BLK)
                    to = {"mk": stA, "mv": mv, "sq": stB, "rv": rv, "mq": stA, "rg": srg,
                          "gs": gates, "gr": gates, "gm": gates, "rq": stB, "rk": stB}
                    if kind in ("us", "ur", "um", "wo"):
                        return
                    if chunk == "mk0":
                        act.wait_ge(rstd_mem_ready, l + 1)
                        act.wait_ge(memt_lo, l + 1)
                    if chunk == "sq0":
                        act.wait_ge(rstd_ready, l * 3 + 2)
                    if kind == "rk":
                        cols = slice(BLK, 2 * BLK)
                    for t in range(TT):
                        name = f"{chunk}t{t}"
                        act.wait_ge(*full(l, name))
                        if kind == "gr":
                            act.wait_ge(*out_of(l, f"us{half}t{t}"))
                        if kind == "gm":
                            act.wait_ge(gates_used, l * 8 + (TT * half + t + 1))
                        if kind == "sk":
                            k = bank(name)[:, 0:SWA_KV * HD].rearrange("p (g d) -> p g d", g=SWA_KV)
                            for dup in range(2):
                                nc.scalar.activation(skd[:, t, :, dup, :], k, ACT.Copy, scale=rstd[:, t:t + 1])
                            scaled(sv[:, t, :], chunk, t, rstd, cols=(P, 2 * P)).then_inc(free(name), 1)
                        else:
                            func = ACT.Silu if kind == "rg" else ACT.Sigmoid if kind[0] == "g" else ACT.Copy
                            scaled(to[kind][:, t, cols], chunk, t, rstd_mem if kind in ("mk", "mv") else rstd,
                                   func).then_inc(free(name), 1)

                def copy_out(name, dst):
                    act.wait_ge(*full(l, name))
                    nc.scalar.activation(dst, bank(name)[:, :], ACT.Copy).then_inc(free(name), 1)

                def two(buf, j):
                    return buf[:, 2 * j:2 * j + 2, :].rearrange("p k t -> p (k t)")

                def step(s):
                    if s in ("xt0", "xt1"):
                        for j in range(2):
                            hi_parts(l, f"{s}_{j}", hT_hi, UB * int(s[2]) + 2 * j, G_MIX)
                        if s == "xt1":
                            act_x_squares(l, 1)
                    elif s == "yt0":
                        for j in range(2):
                            hi_parts(l, f"y0_{j}", hT_hi, 2 * j, G_FFN2)
                    elif s in ("mg0", "mg1"):
                        for j in range(2):
                            hi_parts(l, f"{s}_{j}", hT_hi, UB * int(s[2]) + 2 * j, None)
                    elif s in SPLIT_TO:
                        gain, hi, _ = SPLIT_TO[s]
                        for j in range(4):
                            hi_parts(l, f"{s}_{j}", hi, 2 * j, gain)
                    elif s == "sqt":
                        for j in range(4):
                            copy_out(f"sqt_{j}", two(sqT, j))
                    elif s == "skt":
                        copy_out("skt_0", skT[:, :, :].rearrange("p g t -> p (g t)"))
                    elif s == "mkt":
                        for j in range(4):
                            copy_out(f"mkt_{j}", two(mkT, j))
                    elif s == "mqt":
                        for j in range(4):
                            copy_out(f"mqt_{j}", two(mqT, j))
                    elif s == "rqt":
                        for j in range(2):
                            copy_out(f"rqt_{j}", two(rqT, j))
                    elif s == "rkt":
                        act.wait_ge(rotated, l * 4 + 4)
                        for j in range(2):
                            copy_out(f"rkt_{j}", two(rkT, j))
                    elif s[0] == "e":
                        g = int(s[1])
                        act.wait_ge(swa_max, l * NGRP + (g + 1))
                        nc.scalar.activation(sexp[:, g % 2], ssink[:, g % 2], ACT.Exp)
                        for i in range(GRP):
                            for b in range(2):
                                p = prob[:, g % 2, i, (0 if b == 0 else WIN):(WIN if b == 0 else 3 * WIN)]
                                last = nc.scalar.activation(p, p, ACT.Exp, bias=snm[:, g % 2, i, b:b + 1],
                                                            accum_out=ssum[:, g % 2, i, b:b + 1])
                        last.then_inc(swa_exp, 1)
                    elif s in ("pt0", "pt1", "pt2", "pt3"):
                        for j in range(3):
                            copy_out(f"{s}_{j}", pT[:, 4 * j:4 * j + 4, :].rearrange("p a b -> p (a b)"))
                    elif s == "ro":
                        for h in range(RET_H):
                            act.wait_ge(*full(l, f"ro_{h}"))
                            for t in range(TT):
                                nc.scalar.activation(junk[:, t, h * RET_DV:(h + 1) * RET_DV], bank(f"ro_{h}")[:, t * RET_DV:(t + 1) * RET_DV],
                                                     ACT.Square, scale=RET_DV ** -0.5, accum_out=msq_r[:, 2 * h + t:2 * h + t + 1])\
                                    .then_inc(retsq_ready, 1)
                    elif s == "me":
                        for h in range(MEM_H):
                            act.wait_ge(mem_max, l * MEM_H + (h + 1))
                            for t in range(TT):
                                last = nc.scalar.activation(mprob[:, h, t, :], bank(f"ms_{h}")[:, t * MEM:(t + 1) * MEM],
                                                            ACT.Exp, bias=mnm[:, h, t:t + 1], scale=MEM_HD ** -0.5,
                                                            accum_out=msum[:, h, t:t + 1])
                            last.then_inc(free(f"ms_{h}"), 1)
                    elif s == "mpt":
                        for h in range(MEM_H):
                            copy_out(f"mpt_{h}", mpT[:, h, :, :].rearrange("p m t -> p (m t)"))

                for s in STEPS:
                    if s[0] == "step":
                        step(s[1])
                        continue
                    _, i, chunk, _, last, inside = s
                    for name in inside:
                        step(name)
                    if last:
                        evacuate(chunk)
                    split(l, MIX_AT + i + RING)
                ffn(l, 2, FFN2_AT, G_FFN2)
            act_x_squares(DEPTH, 0)
            act.dma_start(gfin[:, :], gfin_in).then_inc(gfin_loaded, 16)

        @block.vector
        def _(dve):
            n = [0]

            def split(l, unit, uc=0):
                s = unit % RING
                dve.wait_ge(hi_split, l * NU + uc * RING + (unit + 1))
                nc.vector.tensor_tensor(w_lo[:, s], raw[:, s], w_hi[:, s].bitcast(F32), ALU.subtract).then_inc(lo_split, 1)

            def split_on(l, f, unit):
                if f == 1:
                    split(l, unit)
                else:
                    with dve.If(l < DEPTH - 1):
                        split(l, unit)

            def lo_parts(l, name, hi, lo, k0, gain, c=0):
                dve.wait_ge(*hi_out(l, name, c))
                if gain is None:
                    nc.vector.tensor_tensor(lo[:, k0:k0 + 2, :].rearrange("p k t -> p (k t)"), bank(name)[:, :],
                                            hi[:, k0:k0 + 2, :].bitcast(F32).rearrange("p k t -> p (k t)"),
                                            ALU.subtract).then_inc(free(name), 1)
                    return
                for j in range(2):
                    k = k0 + j
                    i = nc.vector.scalar_tensor_tensor(lo[:, k, :], bank(name)[:, j * SEQ:(j + 1) * SEQ],
                                                       cur[:, gain + k:gain + k + 1], hi[:, k, :].bitcast(F32),
                                                       op0=ALU.mult, op1=ALU.subtract)
                i.then_inc(free(name), 1)

            def ffn(l, f, at, gain):
                if f == 1:
                    for j in range(2):
                        lo_parts(l, f"x0_{j}", hT_hi, hT_lo, 2 * j, gain)
                    split(l, RING - 1)
                for j in range(2):
                    lo_parts(l, "xy"[f - 1] + f"1_{j}", hT_hi, hT_lo, UB + 2 * j, gain)
                split(l, at + 3)
                dve.wait_ge(rstd_ready, l * 3 + (1 if f == 1 else 3))

                def times(c):
                    for t in range(TT):
                        up = f"up{f}" + ("" if t == 0 else "t1")
                        dve.wait_ge(silu_ready[t], l * 2 * NCH + c + ((f - 1) * NCH + 1))
                        nc.vector.scalar_tensor_tensor(act_g[:, t, :], bank(up)[:, FC:2 * FC], rstd[:, t:t + 1],
                                                       act_s[:, t, :], op0=ALU.mult, op1=ALU.mult).then_inc(free(up), 1)

                times(0)
                split(l, at + 4)
                if f == 1:
                    dve.wait_ge(memt_hi, l + 1)
                    for k in range(KT):
                        i = nc.vector.scalar_tensor_tensor(bT_lo[:, k, :], memT[:, k, :],
                                                           cur[:, G_MEM + k:G_MEM + k + 1], bT_hi[:, k, :].bitcast(F32),
                                                           op0=ALU.mult, op1=ALU.subtract)
                    i.then_inc(memt_lo, 1)
                with dve.Fori(0, NCH - 2) as c:
                    lo_parts(l, f"gt{f}", gT_hi, gT_lo, 0, None, c)
                    split(l, at + 5, c)
                    times(c + 1)
                    split(l, at + 6, c)
                    split(l, at + 7, c)
                c = NCH - 2
                lo_parts(l, f"gt{f}", gT_hi, gT_lo, 0, None, c)
                split(l, at + 5 + 3 * c)
                times(c + 1)
                split_on(l, f, at + 6 + 3 * c)
                lo_parts(l, f"gt{f}", gT_hi, gT_lo, 0, None, c + 1)
                split_on(l, f, at + 7 + 3 * c)
                for h in range(2):
                    for t in range(TT):
                        nm = f"down{f}_{h}{t}"
                        dve.wait_ge(*full(l, nm))
                        xs = x[:, t, h * BLK:(h + 1) * BLK]
                        nc.vector.scalar_tensor_tensor(xs, bank(nm)[:, :], 0.5, xs, op0=ALU.mult, op1=ALU.add)\
                            .then_inc(free(nm), 1)
                if f == 1:
                    split(l, at + 8 + 3 * c)

            dve.wait_ge(consts_loaded, 16 * 2)
            dve.wait_ge(x_loaded, 16)
            for u in range(RING - 1):
                split(0, u)
            with dve.Fori(0, DEPTH) as l:
                n[0] = 0

                def own(i):
                    n[0] += 1
                    return i.then_inc(dve_step, 1)

                def settled():
                    dve.wait_ge(dve_step, l * DVE_STEPS + n[0])

                nc.vector.tensor_copy(cur[:, :], gains[:, bass.ds(l, 1), :].rearrange("p a g -> p (a g)"))\
                    .then_inc(layer_consts, 1)
                dve.wait_ge(layer_consts, l + 1)
                ffn(l, 1, 0, G_FFN1)

                dve.wait_ge(tables_loaded, 16 * 3)

                def evacuate(chunk):
                    kind, half = chunk[:2], chunk[2]
                    if kind not in ("us", "ur", "um", "wo"):
                        return
                    half = int(half)
                    for t in range(TT):
                        name = f"{chunk}t{t}"
                        dve.wait_ge(*full(l, name))
                        cols = slice(half * BLK, (half + 1) * BLK)
                        g, m = gates[:, t, cols], merged[:, t, cols]
                        if kind == "wo":
                            xs = x[:, t, cols]
                            nc.vector.tensor_tensor(xs, bank(name)[:, :], xs, ALU.add)\
                                .then_inc(free(name), 1)
                            continue
                        gate = {"us": "gs", "ur": "gr", "um": "gm"}[kind] + f"{half}t{t}"
                        dve.wait_ge(*out_of(l, gate))
                        if kind == "us":
                            nc.vector.tensor_tensor(m, bank(name)[:, :], g, ALU.mult).then_inc(free(name), 1)
                        else:
                            nc.vector.tensor_tensor(g, bank(name)[:, :], g, ALU.mult).then_inc(free(name), 1)
                            dve.wait_ge(*out_of(l, name))
                            nc.vector.tensor_tensor(m, m, g, ALU.add).then_inc(gates_used, 1)

                def step(s):
                    if s in ("xt0", "xt1"):
                        for j in range(2):
                            lo_parts(l, f"{s}_{j}", hT_hi, hT_lo, UB * int(s[2]) + 2 * j, G_MIX)
                    elif s == "yt0":
                        for j in range(2):
                            lo_parts(l, f"y0_{j}", hT_hi, hT_lo, 2 * j, G_FFN2)
                    elif s in ("mg0", "mg1"):
                        for j in range(2):
                            lo_parts(l, f"{s}_{j}", hT_hi, hT_lo, UB * int(s[2]) + 2 * j, None)
                    elif s in SPLIT_TO:
                        gain, hi, lo = SPLIT_TO[s]
                        for j in range(4):
                            lo_parts(l, f"{s}_{j}", hi, lo, 2 * j, gain)
                    elif s in ("s0", "s1", "s2", "s3"):
                        g = int(s[1])
                        pr, par = prob[:, g % 2], g % 2
                        for j in range(4):
                            name, (b, odd) = f"s{g}_{j}", divmod(j, 2)
                            w = WIN * (b + 1)
                            src = bank(name)[:, 0:2 * w].rearrange("p (h k) -> p h k", h=2)
                            dst = pr[:, odd::2, 0:WIN] if b == 0 else pr[:, odd::2, WIN:3 * WIN]
                            msk = (mask[:, WIN:] if b == 0 else mask[:, :]).unsqueeze(1).broadcast_to([P, 2, w])
                            dve.wait_ge(*full(l, name))
                            nc.vector.scalar_tensor_tensor(dst, src, HD ** -0.5, msk, op0=ALU.mult, op1=ALU.add)\
                                .then_inc(free(name), 1)
                        for j in range(4):
                            dve.wait_ge(*out_of(l, f"s{g}_{j}"))
                        nc.vector.tensor_reduce(smax[:, par, :, 0], pr[:, :, 0:WIN], axis=AXX, op=ALU.max)
                        own(nc.vector.tensor_reduce(smax[:, par, :, 1], pr[:, :, WIN:3 * WIN], axis=AXX, op=ALU.max))
                        settled()
                        sink = cur[:, G_SINK + GRP * g:G_SINK + GRP * (g + 1)].unsqueeze(2).broadcast_to([P, GRP, 2])
                        own(nc.vector.tensor_tensor(smax[:, par], smax[:, par], sink, ALU.max))
                        settled()
                        nc.vector.tensor_scalar(snm[:, par], smax[:, par], -1.0, None, ALU.mult)
                        nc.vector.tensor_tensor(ssink[:, par], sink, smax[:, par], ALU.subtract).then_inc(swa_max, 1)
                    elif s in ("pv0", "pv1", "pv2", "pv3"):
                        g = int(s[2])
                        par = g % 2
                        dve.wait_ge(swa_exp, l * NGRP + (g + 1))
                        own(nc.vector.tensor_tensor(ssum[:, par], ssum[:, par], sexp[:, par], ALU.add))
                        settled()
                        own(nc.vector.reciprocal(ssum[:, par], ssum[:, par]))
                        settled()
                        name = f"pv{g}_0"
                        dve.wait_ge(*full(l, name))
                        for t in range(TT):
                            o = bank(name)[:, :].rearrange("p (h b d) -> p h b d", h=GRP, b=2)[:, :, t, :]
                            dst = stA[:, t, GRP * HD * g:GRP * HD * (g + 1)].rearrange("p (h d) -> p h d", h=GRP)
                            i = nc.vector.tensor_tensor(dst, o, ssum[:, par, :, t:t + 1].broadcast_to([P, GRP, HD]), ALU.mult)
                        i.then_inc(free(name), 1)
                    elif s == "rs":
                        for h in range(RET_H):
                            name = f"rs_{h}"
                            dve.wait_ge(*full(l, name))
                            nc.vector.tensor_tensor(sdec[:, h, 0:2 * P], bank(name)[:, 0:2 * P], decay[:, h, :], ALU.mult)
                            nc.vector.tensor_tensor(sdec[:, h, 2 * P:], bank(name)[:, 2 * P:3 * P], decay[:, h, 0:P],
                                                    ALU.mult).then_inc(free(name), 1)
                    elif s == "re":
                        dve.wait_ge(retstd_ready, l + 1)
                        for t in range(TT):
                            dve.wait_ge(*out_of(l, f"rg1t{t}"))
                        for h in range(RET_H):
                            name = f"ro_{h}"
                            for t in range(TT):
                                cols = slice(h * RET_DV, (h + 1) * RET_DV)
                                i = nc.vector.scalar_tensor_tensor(stB[:, t, cols], bank(name)[:, t * RET_DV:(t + 1) * RET_DV],
                                                                   rstd_r[:, 2 * h + t:2 * h + t + 1], srg[:, t, cols],
                                                                   op0=ALU.mult, op1=ALU.mult)
                            i.then_inc(free(name), 1)
                    elif s == "ms":
                        for h in range(MEM_H):
                            name = f"ms_{h}"
                            dve.wait_ge(*full(l, name))
                            own(nc.vector.tensor_reduce(mmax[:, h, :], bank(name)[:, :].rearrange("p (t m) -> p t m", t=TT),
                                                        axis=AXX, op=ALU.max))
                            settled()
                            nc.vector.tensor_scalar(mnm[:, h, :], mmax[:, h, :], -(MEM_HD ** -0.5), None, ALU.mult)\
                                .then_inc(mem_max, 1)
                    elif s == "mpv":
                        for h in range(MEM_H):
                            dve.wait_ge(*out_of(l, f"ms_{h}"))
                        own(nc.vector.reciprocal(msum[:, :, :], msum[:, :, :]))
                        settled()
                        for h in range(MEM_H):
                            name = f"mpv_{h}"
                            dve.wait_ge(*full(l, name))
                            for t in range(TT):
                                i = nc.vector.tensor_scalar(stB[:, t, h * MEM_HD:(h + 1) * MEM_HD],
                                                            bank(name)[:, t * MEM_HD:(t + 1) * MEM_HD],
                                                            msum[:, h, t:t + 1], None, ALU.mult)
                            i.then_inc(free(name), 1)

                for s in STEPS:
                    if s[0] == "step":
                        step(s[1])
                        continue
                    _, i, chunk, _, last, inside = s
                    for name in inside:
                        step(name)
                    if last:
                        evacuate(chunk)
                    split(l, MIX_AT + i + RING)
                ffn(l, 2, FFN2_AT, G_FFN2)
                assert n[0] == DVE_STEPS, n
            dve.wait_ge(rstd_ready, DEPTH * 3 + 1)
            dve.wait_ge(gfin_loaded, 16)
            for t in range(TT):
                nc.vector.scalar_tensor_tensor(stB[:, t, :], x[:, t, :], rstd[:, t:t + 1], gfin[:, :],
                                               op0=ALU.mult, op1=ALU.mult).then_inc(final_ready, 1)


def _ffn_units(w1, w3, w2):
    up = np.stack([w1.reshape(KT, P, NCH, FC), w3.reshape(KT, P, NCH, FC)], axis=3)
    up = up.transpose(2, 0, 1, 3, 4).reshape(NCH, 2, UB, P, BLK).transpose(0, 1, 3, 2, 4).reshape(NCH, 2, P, UW)
    down = w2.reshape(NCH, 2, P, 2, BLK).transpose(0, 2, 3, 1, 4).reshape(NCH, P, UW)
    units = list(up[0])
    for c in range(NCH - 1):
        units += [*up[c + 1], down[c]]
    return units + [down[NCH - 1]]


def _mix_units(w_in, w_kv, w_ur, w_us, w_um, w_o):
    units = []
    for c, u, _ in UNITS:
        kind, half = c[:2], c[2]
        if c == "skv":
            at = W_IN_AT["skv"]
            units.append(w_in[:, at:at + 256].reshape(KT, P, 256).transpose(1, 0, 2).reshape(P, UW))
            continue
        at = int(half) * BLK
        if kind in ("mk", "mv"):
            w, at = w_kv, at + (D if kind == "mv" else 0)
        elif kind in ("us", "ur", "um", "wo"):
            w = {"us": w_us, "ur": w_ur, "um": w_um, "wo": w_o}[kind]
        elif kind[0] == "g":
            w, at = w_in, W_IN_AT["gl"] + "rsm".index(kind[1]) * D + at
        else:
            w, at = w_in, W_IN_AT[kind] + at
        units.append(w[u * UB * P:(u + 1) * UB * P, at:at + BLK].reshape(UB, P, BLK).transpose(1, 0, 2).reshape(P, UW))
    return units


def _tables():
    f = np.float32
    half = RET_DK // 2
    inv = f(10000.0) ** (-np.arange(half, dtype=f) / f(half))
    ang = np.arange(SEQ, dtype=f)[:, None] * inv[None, :]
    cos, sin = np.cos(ang), np.sin(ang)
    rot = np.stack([np.concatenate([cos, cos], 1), np.concatenate([-sin, sin], 1)])
    rot = rot.reshape(2, TT, P, P).transpose(2, 0, 1, 3)
    log_g = np.log1p(-(f(2.0) ** (f(-5.0) - np.arange(RET_H, dtype=f)))).astype(f)
    i = np.arange(P, dtype=f)
    diff = i[None, :] - i[:, None]
    own = np.where(diff[None] >= 0, np.exp(np.maximum(diff, f(0))[None] * log_g[:, None, None]), f(0))
    cross = np.exp((diff[None] + f(P)) * log_g[:, None, None])
    decay = (np.concatenate([own, cross], 2) * f(RET_DK ** -0.5)).transpose(1, 0, 2)
    rel = np.arange(WIN)[:, None] + WIN - np.arange(2 * WIN)[None, :]
    mask = np.where((rel >= 0) & (rel < WIN), f(0), f(-1e30))
    return [np.ascontiguousarray(a.astype(f)) for a in (rot, decay, mask, np.eye(P, dtype=f))]


def kernel(x, mem, norm_ffn1, ffn1_w1, ffn1_w3, ffn1_w2, norm_mix, w_in, ret_gn, swa_sinks, norm_mem, w_mem_kv,
           w_up_ret, w_up_swa, w_up_mem, w_o, norm_ffn2, ffn2_w1, ffn2_w3, ffn2_w2, norm_final):
    import concourse.bacc as bacc
    from concourse.bass_utils import run_bass_kernel_spmd

    a = {k: np.asarray(v) for k, v in locals().items() if k not in ("bacc", "run_bass_kernel_spmd")}
    units = []
    for l in range(DEPTH):
        units += _ffn_units(a["ffn1_w1"][l], a["ffn1_w3"][l], a["ffn1_w2"][l])
        units += _mix_units(*(a[n][l] for n in ("w_in", "w_mem_kv", "w_up_ret", "w_up_swa", "w_up_mem", "w_o")))
        units += _ffn_units(a["ffn2_w1"][l], a["ffn2_w3"][l], a["ffn2_w2"][l])
    gains = np.stack([np.concatenate(
        [a[n][l].reshape(KT, P).T for n in ("norm_ffn1", "norm_mix", "norm_mem", "ret_gn", "norm_ffn2")]
        + [np.broadcast_to(a["swa_sinks"][l], (P, SWA_H))], axis=1) for l in range(DEPTH)], axis=1)
    rot, decay, mask, ident = _tables()
    arrays = {
        "x": a["x"][0], "mem": a["mem"][0], "memt": a["mem"][0].T.reshape(KT, P, MEM).transpose(1, 0, 2),
        "stream": np.stack(units), "gains": gains, "gfin": np.broadcast_to(a["norm_final"], (P, D)),
        "rot": rot, "decay": decay, "mask": mask, "ident": ident,
    }
    nc = bacc.Bacc("TRN2", target_bir_lowering=False, num_devices=1)
    arrays = {f"in_{k}": np.ascontiguousarray(v) for k, v in arrays.items()}
    args = [nc.dram_tensor(k, v.shape, mybir.dt.from_np(v.dtype), kind="ExternalInput").ap() for k, v in arrays.items()]
    out = nc.dram_tensor("out", (SEQ, D), F32, kind="ExternalOutput").ap()
    build(nc, *args, out)
    got = run_bass_kernel_spmd(nc, [arrays], core_ids=[0]).results[0]["out"]
    return got.reshape(a["x"].shape)
```

```python
from contextlib import ExitStack

import numpy as np

import concourse.bass as bass
from concourse import mybir

F32 = mybir.dt.float32
F32R = mybir.dt.float32r
BF16 = mybir.dt.bfloat16
ACT = mybir.ActivationFunctionType
ALU = mybir.AluOpType
AXX = mybir.AxisListType.X

P = 128
D = 1024
SEQ = 256
MEM = 256
DEPTH = 2
EPS = 1e-6
DFF = 2816
KT = D // P
TT = SEQ // P
BLK = 512
UB = 4
UW = UB * BLK
FC = 256
NCH = DFF // FC
RING = 3

RET_H, RET_DK, RET_DV = 4, 128, 256
SWA_H, SWA_KV, HD, WIN = 16, 2, 64, 128
GRP = 4
NGRP = SWA_H // GRP
MEM_H, MEM_HD = 4, 256

W_IN_AT = {"rq": 0, "rk": 512, "rv": 1024, "rg": 2048, "sq": 3072, "skv": 4096, "mq": 4352, "gl": 5376}
CHUNKS = ["mk0", "sq0", "sq1", "skv", "mk1", "mv0", "mv1", "rq0", "rk0", "rv0", "rv1", "rg0", "rg1",
          "gs0", "gs1", "us0", "us1", "mq0", "mq1", "gr0", "gr1", "ur0", "ur1", "gm0", "gm1", "um0",
          "um1", "wo0", "wo1"]
FFN_UNITS = 3 * NCH
MIX_UNITS = 2 * len(CHUNKS) - 1
NU = 2 * FFN_UNITS + MIX_UNITS
MIX_AT = FFN_UNITS
FFN2_AT = FFN_UNITS + MIX_UNITS
assert NU % RING == 0 and MIX_AT % RING == 0 and FFN2_AT % RING == 0

UNITS = [(c, u, u == (c != "skv")) for c in CHUNKS[:-2] for u in range(1 if c == "skv" else 2)]
UNITS += [(c, u, u == 1) for u in range(2) for c in CHUNKS[-2:]]

AFTER = {7: ["sqt"], 8: ["skt"], 9: ["s0"], 10: ["mkt"], 11: ["e0"], 12: ["s1"],
         13: ["pt0"], 14: ["pv0", "e1"], 15: ["s2"], 16: ["pt1"], 17: ["pv1", "e2"], 18: ["s3"],
         19: ["pt2"], 20: ["pv2", "e3"], 21: ["rqt", "rkt"], 22: ["pt3"], 23: ["pv3"], 24: ["rs"],
         26: ["st"], 27: ["ro"], 29: ["re"], 33: ["rt"],
         38: ["mqt"], 40: ["ms"], 41: ["me", "mn"], 43: ["mpt"], 45: ["mpv"],
         51: ["mg0"], 53: ["mg1"]}
INSIDE = {1: ["xt0"], 2: ["xt1"], 56: ["yt0"]}
STEPS = []
for _i, _u in enumerate(UNITS):
    STEPS.append(("unit", _i, *_u, INSIDE.get(_i, [])))
    STEPS += [("step", s) for s in AFTER.get(_i, [])]

FIRST_MIX, LAST_DOWN = MIX_AT - 1, MIX_AT
FFN_ENDS = [u in (1, FFN_UNITS - 1) or (1 < u and u % RING == 0) for u in range(FFN_UNITS)]
ENDS = FFN_ENDS + [last for *_, last in UNITS] + FFN_ENDS
ENDS[FIRST_MIX], ENDS[LAST_DOWN] = ENDS[LAST_DOWN], ENDS[FIRST_MIX]
USED = [ENDS[:u + 1].count(False) for u in range(NU)]
USED_TURN = 2

G_FFN1, G_MIX, G_MEM, G_RET, G_FFN2 = (KT * i for i in range(5))
G_SINK = 5 * KT
NG = G_SINK + SWA_H
DVE_STEPS = 24


class Banks:

    def __init__(self):
        self.uses, self.hi, self.at = [0] * 8, [0] * 8, {}

    def add(self, name, bank, n=1, split=False):
        self.at[name] = (bank, self.uses[bank], self.hi[bank])
        self.uses[bank] += n
        self.hi[bank] += n * split


def plan_banks():
    banks = Banks()

    def ffn(f):
        for t in range(TT):
            banks.add(f"up{f}_0t{t}", 2 + t)
            banks.add(f"up{f}t{t}", 4 + t, NCH - 1)
        banks.add(f"gt{f}", 6, NCH, split=True)
        for h in range(2):
            for t in range(TT):
                banks.add(f"down{f}_{h}{t}", 2 * h + t)

    def xt(name, bank):
        for j in range(2):
            banks.add(f"{name}_{j}", bank + j, split=True)

    xt("x0", 6)
    xt("x1", 4)
    ffn(1)
    for t in range(TT):
        banks.add(f"mk0t{t}", 4 + t)
    turn = [2]

    def take(name, n, split=False):
        for j in range(n):
            banks.add(f"{name}_{j}", 4 + turn[0] % 4, split=split)
            turn[0] += 1

    sizes = {"xt0": (2, True), "xt1": (2, True), "sqt": (4, False), "skt": (1, False), "mkt": (4, False),
             "st": (4, True), "rqt": (2, False), "rkt": (2, False), "rs": (4, False), "ro": (4, False),
             "rt": (4, True), "mqt": (4, False), "ms": (4, False), "mpt": (4, False), "mpv": (4, True),
             "mg0": (2, True), "mg1": (2, True)}
    sizes |= {f"s{g}": (4, False) for g in range(NGRP)}
    sizes |= {f"pt{g}": (3, False) for g in range(NGRP)} | {f"pv{g}": (1, False) for g in range(NGRP)}
    for s in STEPS:
        if s[0] == "unit":
            _, _, chunk, u, _, inside = s
            for name in inside:
                xt("y0", 6) if name == "yt0" else take(name, *sizes[name])
            if u == 0 and chunk != "mk0":
                for t in range(TT):
                    banks.add(f"{chunk}t{t}", 2 * (CHUNKS.index(chunk) % 2) + t)
        elif s[1] in sizes:
            take(s[1], *sizes[s[1]])
    xt("y1", 6)
    ffn(2)
    return banks


def build(nc, x_in, mem_in, memt_in, stream, gains_in, gfin_in, rot_in, decay_in, mask_in, ident_in, out):
    banks = plan_banks()
    where, USES, HIS = banks.at, banks.uses, banks.hi

    ctx = ExitStack()
    with ctx:
        top = [nc.sbuf_base]

        def place(name, shape, dt=F32, at=None):
            size = int(np.prod(shape[1:])) * (2 if dt == BF16 else 4)
            if at is None:
                top[0] = -(-top[0] // 32) * 32
                at, top[0] = top[0], top[0] + size
            return nc.alloc_sbuf_tensor_at(name, shape, dt, offset=at), at

        def new(name, shape, dt=F32, at=None):
            return place(name, shape, dt, at)[0]

        x = new("x", [P, TT, D])
        hT_hi = new("hT_hi", [P, KT, SEQ], F32R)
        hT_lo = new("hT_lo", [P, KT, SEQ], F32R)
        raw = new("raw", [P, RING, UW])
        w_hi = new("w_hi", [P, RING, UW], F32R)
        w_lo = new("w_lo", [P, RING, UW], F32R)
        bT_hi = new("bT_hi", [P, KT, SEQ], F32R)
        bT_lo = new("bT_lo", [P, KT, SEQ], F32R)
        stA, a_at = place("stA", [P, TT, D])
        memT = new("memT", [P, KT, MEM], at=a_at)
        gfin = new("gfin", [P, D], at=a_at)
        stB, b_at = place("stB", [P, TT, D])
        mkT = new("mkT", [P, KT, MEM])
        mv = new("mv", [P, TT, D])
        rqT, q_at = place("rqT", [P, RET_H, SEQ])
        rkT, k_at = place("rkT", [P, RET_H, SEQ])
        rot_a = new("rot_a", [P, BLK], at=k_at)
        rot_b = new("rot_b", [P, BLK], at=k_at + 4 * BLK)
        mqT = new("mqT", [P, KT, SEQ], at=q_at)
        rv, v_at = place("rv", [P, TT, D])
        merged = new("merged", [P, TT, D], at=v_at)
        srg, s_at = place("srg", [P, TT, D])
        mpT = new("mpT", [P, MEM_H, TT, SEQ], at=s_at)
        sqT, sq_at = place("sqT", [P, KT, SEQ])
        gates = new("gates", [P, TT, D], at=sq_at)
        skT = new("skT", [P, SWA_KV, SEQ])
        sv = new("sv", [P, TT, P])
        prob, p_at = place("prob", [P, 2, GRP, 3 * WIN])
        mprob = new("mprob", [P, MEM_H, TT, MEM], at=p_at)
        sdec = new("sdec", [P, RET_H, 3 * P], at=p_at)
        act_s = new("act_s", [P, TT, FC], at=p_at)
        act_g = new("act_g", [P, TT, FC], at=p_at + 2048)
        gT_hi = new("gT_hi", [P, 2, SEQ], F32R, at=p_at + 4096)
        gT_lo = new("gT_lo", [P, 2, SEQ], F32R, at=p_at + 6144)
        junk = new("junk", [P, TT, D], BF16, at=p_at + 8192)
        pT, pt_at = place("pT", [P, 3 * GRP, P])
        skd = new("skd", [P, TT, SWA_KV, 2, HD], at=pt_at)
        rot = new("rot", [P, 2, TT, P])
        decay = new("decay", [P, RET_H, 2 * P])
        mask = new("mask", [P, 2 * WIN])
        ident = new("ident", [P, P])
        gains = new("gains", [P, DEPTH, NG])
        cur = new("cur", [P, NG])
        msq = new("msq", [P, TT])
        rstd = new("rstd", [P, TT])
        msq_end = new("msq_end", [P, 2, TT])
        msq_mem = new("msq_mem", [P, TT])
        rstd_mem = new("rstd_mem", [P, TT])
        msq_r = new("msq_r", [P, 2 * RET_H])
        rstd_r = new("rstd_r", [P, 2 * RET_H])
        eps = new("eps", [P, 2 * RET_H])
        mhalf = new("mhalf", [P, 2 * RET_H])
        smax = new("smax", [P, 2, GRP, 2])
        snm = new("snm", [P, 2, GRP, 2])
        ssink = new("ssink", [P, 2, GRP, 2])
        sexp = new("sexp", [P, 2, GRP, 2])
        ssum = new("ssum", [P, 2, GRP, 2])
        mmax = new("mmax", [P, MEM_H, TT])
        mnm = new("mnm", [P, MEM_H, TT])
        msum = new("msum", [P, MEM_H, TT])
        assert top[0] <= nc.sbuf_usable_end, top

        ps = [ctx.enter_context(nc.psum_tensor(f"bank{b}", [P, BLK], F32)) for b in range(8)]

        def sem(name):
            return ctx.enter_context(nc.semaphore(name))

        raw_loaded = [sem(f"raw_loaded{s}") for s in range(RING)]
        hi_split, lo_split, unit_used = sem("hi_split"), sem("lo_split"), sem("unit_used")
        psum_full = [sem(f"psum_full{b}") for b in range(8)]
        psum_hi = [sem(f"psum_hi{b}") for b in range(8)]
        psum_free = [sem(f"psum_free{b}") for b in range(8)]
        x_loaded = [sem(f"x_loaded{h}") for h in range(2)]
        consts_loaded, tables_loaded, mem_loaded, memt_loaded = map(
            sem, ["consts_loaded", "tables_loaded", "mem_loaded", "memt_loaded"])
        layer_consts, memt_hi, memt_lo = map(sem, ["layer_consts", "memt_hi", "memt_lo"])
        msq_ready, rstd_ready, mem_msq_ready, rstd_mem_ready = map(sem, ["msq_ready", "rstd_ready", "mem_msq_ready", "rstd_mem_ready"])
        rotated, pool_step, dve_step, gates_used = map(sem, ["rotated", "pool_step", "dve_step", "gates_used"])
        swa_max, swa_exp, retsq_ready, retstd_ready, mem_max, mem_probs = map(
            sem, ["swa_max", "swa_exp", "retsq_ready", "retstd_ready", "mem_max", "mem_probs"])
        silu_ready = [sem(f"silu_ready{t}") for t in range(TT)]
        gfin_loaded, end_msq, final_ready, out_stored = map(sem, ["gfin_loaded", "end_msq", "final_ready", "out_stored"])

        def full(l, name, c=0):
            b, i, _ = where[name]
            return psum_full[b], l * USES[b] + c + (i + 1)

        def room(l, name, c=0):
            b, i, _ = where[name]
            return psum_free[b], l * USES[b] + c + (i + 1)

        def out_of(l, name, c=0):
            b, i, _ = where[name]
            return psum_free[b], l * USES[b] + c + (i + 2)

        def hi_out(l, name, c=0):
            b, _, j = where[name]
            return psum_hi[b], l * HIS[b] + c + (j + 1)

        def used(l, unit, c=0):
            if not ENDS[unit]:
                return unit_used, l * USED[-1] + c * USED_TURN + USED[unit]
            if unit < MIX_AT or unit >= FFN2_AT:
                f, at = (1, 0) if unit < MIX_AT else (2, FFN2_AT)
                if unit - at == FFN_UNITS - 1:
                    return full(l, f"down{f}_11")
                if unit - at == 1:
                    return full(l, f"up{f}_0t1")
                return full(l, f"up{f}t1", c + ((unit - at) // RING - 1))
            if unit == LAST_DOWN:
                return full(l, "down1_11")
            return full(l, UNITS[unit - MIX_AT][0] + "t1")

        def bank(name):
            return ps[where[name][0]]

        def free(name):
            return psum_free[where[name][0]]

        def fullsem(name):
            return psum_full[where[name][0]]

        def hisem(name):
            return psum_hi[where[name][0]]

        def x_of_layer_before(eng, l, b):
            eng.wait_ge(psum_free[b], l * USES[b] + 1)

        SPLIT_TO = {"rt": (G_RET, bT_hi, bT_lo), "st": (None, bT_hi, bT_lo), "mpv": (None, bT_hi, bT_lo)}

        block = ctx.enter_context(nc.Block())

        @block.sync
        def _(sp):
            for s in range(RING):
                if s < 2:
                    cols = slice(s * BLK, (s + 1) * BLK)
                    sp.dma_start(x[:, :, cols], x_in[:, cols].rearrange("(t p) d -> p t d", p=P)).then_inc(x_loaded[s], 16)
                sp.dma_start(raw[:, s], stream[s]).then_inc(raw_loaded[s], 16)
            with sp.Fori(1, DEPTH * NU // RING) as i:
                for s in range(RING):
                    sp.wait_ge(lo_split, i * RING + (s + 1 - RING))
                    sp.dma_start(raw[:, s], stream[i * RING + s]).then_inc(raw_loaded[s], 16)
            for t in range(TT):
                for h in range(2):
                    cols = slice(h * BLK, (h + 1) * BLK)
                    sp.wait_ge(final_ready, 2 * t + h + 1)
                    sp.dma_start(out[t * P:(t + 1) * P, cols], stB[:, t, cols]).then_inc(out_stored, 16)
            sp.wait_ge(out_stored, 2 * TT * 16)

        @block.gpsimd
        def _(pool):
            pool.wait_ge(x_loaded[1], 16)
            for dst, src in ((rot, rot_in), (decay, decay_in), (mask, mask_in)):
                pool.dma_start(dst[:], src).then_inc(tables_loaded, 16)
            pool.memset(eps[:, :], EPS).then_inc(pool_step, 1)
            pool.memset(mhalf[:, :], -0.5).then_inc(pool_step, 1)
            pool.wait_ge(pool_step, 2)

            def inv_rms(dst, src, n, done, step):
                pool.tensor_tensor(dst[:, 0:n], src[:, 0:n], eps[:, 0:n], ALU.add).then_inc(pool_step, 1)
                pool.wait_ge(pool_step, step)
                pool.tensor_tensor(dst[:, 0:n], dst[:, 0:n], mhalf[:, 0:n], ALU.pow).then_inc(done, 1)

            PER = 5 + 4 * 3
            with pool.Fori(0, DEPTH) as l:
                def at(n):
                    return l * PER + (2 + n)

                pool.wait_ge(msq_ready, l * 3 * TT + TT)
                inv_rms(rstd, msq, TT, rstd_ready, at(1))
                pool.wait_ge(mem_msq_ready, l * TT + TT)
                inv_rms(rstd_mem, msq_mem, TT, rstd_mem_ready, at(2))
                pool.wait_ge(msq_ready, l * 3 * TT + 2 * TT)
                inv_rms(rstd, msq, TT, rstd_ready, at(3))
                pool.wait_ge(tables_loaded, 16 * 3)
                n = 3
                for qk, name in enumerate(("rq0", "rk0")):
                    for t in range(TT):
                        pool.wait_ge(*out_of(l, f"{name}t{t}"))
                        src = stB[:, t, qk * BLK:(qk + 1) * BLK].rearrange("p (h d) -> p h d", h=RET_H)
                        av = rot_a[:, :].rearrange("p (h d) -> p h d", h=RET_H)
                        bv = rot_b[:, :].rearrange("p (h d) -> p h d", h=RET_H)
                        half = RET_DK // 2
                        cos = rot[:, 0, t].unsqueeze(1).broadcast_to([P, RET_H, P])
                        if n > 3:
                            pool.wait_ge(rotated, l * 4 + (qk * TT + t))
                        pool.tensor_tensor(av, src, cos, ALU.mult).then_inc(pool_step, 1)
                        for lo, hi in ((0, half), (half, 0)):
                            sin = rot[:, 1, t, lo:lo + half].unsqueeze(1).broadcast_to([P, RET_H, half])
                            pool.tensor_tensor(bv[:, :, lo:lo + half], src[:, :, hi:hi + half], sin, ALU.mult)\
                                .then_inc(pool_step, 1)
                        n += 3
                        pool.wait_ge(pool_step, at(n))
                        pool.tensor_tensor(src, av, bv, ALU.add).then_inc(rotated, 1)
                pool.wait_ge(retsq_ready, l * 2 * RET_H + 2 * RET_H)
                inv_rms(rstd_r, msq_r, 2 * RET_H, retstd_ready, at(n + 1))
                pool.wait_ge(msq_ready, l * 3 * TT + 3 * TT)
                inv_rms(rstd, msq, TT, rstd_ready, at(n + 2))
                assert n + 2 == PER
            step = DEPTH * PER + 2
            pool.wait_ge(end_msq, TT)
            pool.tensor_tensor(rstd[:, :], msq_end[:, 0, :], eps[:, 0:TT], ALU.add).then_inc(pool_step, 1)
            pool.wait_ge(pool_step, step + 1)
            for t in range(TT):
                r = rstd[:, t:t + 1]
                pool.wait_ge(end_msq, TT + t + 1)
                pool.tensor_tensor(r, r, msq_end[:, 1, t:t + 1], ALU.add).then_inc(pool_step, 1)
                pool.wait_ge(pool_step, step + (t + 2))
                pool.tensor_tensor(r, r, mhalf[:, 0:1], ALU.pow).then_inc(rstd_ready, 1)

        @block.tensor
        def _(pe):
            for b in range(8):
                pe.nop().then_inc(psum_free[b], 1)
            pe.wait_ge(consts_loaded, 16 * 2)

            def three_passes(dst, xh, xl, slot, cols, first, last):
                a, b = cols
                nc.tensor.matmul(dst, xl, w_hi[:, slot, a:b], start=first, stop=False)
                nc.tensor.matmul(dst, xh, w_hi[:, slot, a:b], start=False, stop=False)
                return nc.tensor.matmul(dst, xh, w_lo[:, slot, a:b], start=False, stop=last)

            def tokens(t):
                return slice(t * P, (t + 1) * P)

            def project(l, unit, names, hi, lo, half, c=0, uc=0, inside=None):
                pe.wait_ge(lo_split, l * NU + uc + (unit + 1))
                for t in range(TT):
                    if t == 1 and inside:
                        inside()
                    if half == 0:
                        pe.wait_ge(*room(l, names[t], c))
                    for j in range(UB):
                        k = UB * half + j
                        last = three_passes(bank(names[t])[:, :], hi[:, k, tokens(t)], lo[:, k, tokens(t)],
                                            unit % RING, (j * BLK, (j + 1) * BLK), k == 0, k == KT - 1)
                    if half == 1:
                        last.then_inc(fullsem(names[t]), 1)
                if half == 0:
                    last.then_inc(unit_used, 1)

            def project_kv(l, unit, names):
                pe.wait_ge(lo_split, l * NU + (unit + 1))
                for t in range(TT):
                    pe.wait_ge(*room(l, names[t]))
                    for k in range(KT):
                        last = three_passes(bank(names[t])[:, 0:256], hT_hi[:, k, tokens(t)], hT_lo[:, k, tokens(t)],
                                            unit % RING, (k * 256, (k + 1) * 256), k == 0, k == KT - 1)
                    last.then_inc(fullsem(names[t]), 1)

            def wait_out(l, names, then, c=0):
                last = {where[name][0]: name for name in names}
                for b, name in last.items():
                    if b not in {where[t][0] for t in then}:
                        pe.wait_ge(*out_of(l, name, c))

            def transpose_to(l, name, src, k0, tiles=TT, c=0):
                pe.wait_ge(*room(l, name, c))
                for j in range(2):
                    for t in range(tiles):
                        at = (j * tiles + t) * P
                        last = nc.tensor.transpose(bank(name)[:, at:at + P], src(t, k0 + j), ident[:, :])
                last.then_inc(fullsem(name), 1)

            def token_major(buf):
                return lambda t, k: buf[:, t, k * P:(k + 1) * P]

            def x_transposes(l, name, h):
                for j in range(2):
                    transpose_to(l, f"{name}_{j}", token_major(x), UB * h + 2 * j)

            def ffn(l, f, at):
                up0, up = ([f"up{f}{of}t{t}" for t in range(TT)] for of in ("_0", ""))

                def transpose_g(c, first=False):
                    for t in range(TT):
                        pe.wait_ge(*(out_of(l, up0[t]) if first else out_of(l, up[t], c - 1)))
                    transpose_to(l, f"gt{f}", token_major(act_g), 0, c=c)

                def down(c, uc, unit, first, last_chunk):
                    pe.wait_ge(lo_split, l * NU + uc + (unit + 1))
                    pe.wait_ge(*out_of(l, f"gt{f}", c))
                    for h in range(2):
                        for t in range(TT):
                            name = f"down{f}_{h}{t}"
                            if first:
                                pe.wait_ge(*room(l, name))
                            for j in range(2):
                                i = three_passes(bank(name)[:, :], gT_hi[:, j, tokens(t)], gT_lo[:, j, tokens(t)],
                                                 unit % RING, ((2 * h + j) * BLK, (2 * h + j + 1) * BLK),
                                                 first and j == 0, last_chunk and j == 1)
                            if last_chunk:
                                i.then_inc(fullsem(name), 1)
                    if not last_chunk:
                        i.then_inc(unit_used, 1)

                def half_of_x(h):
                    for t in range(TT):
                        if f == 1:
                            x_of_layer_before(pe, l, 2 * h + t)
                        else:
                            pe.wait_ge(*out_of(l, f"wo1t{t}"))
                    x_transposes(l, "xy"[f - 1] + str(h), h)

                if f == 1:
                    pe.wait_ge(x_loaded[0], 16)
                    half_of_x(0)
                    pe.wait_ge(x_loaded[1], 16)

                for h in range(2):
                    for j in range(2):
                        pe.wait_ge(*out_of(l, "xy"[f - 1] + f"{h}_{j}"))
                    project(l, at + h, up0, hT_hi, hT_lo, h, inside=(lambda: half_of_x(1)) if h == 0 else None)

                def turn(start, i, first):
                    unit = at + 2 + 3 * start
                    project(l, unit, up, hT_hi, hT_lo, 0, i + start, i * 3)
                    transpose_g(i + start, first)
                    project(l, unit + 1, up, hT_hi, hT_lo, 1, i + start, i * 3)
                    down(i + start, i * 3, unit + 2, first, False)

                turn(0, 0, True)
                with pe.Fori(0, NCH - 2) as i:
                    turn(1, i, False)
                transpose_g(NCH - 1)
                if f == 1:
                    pe.wait_ge(memt_lo, l + 1)
                    project(l, FIRST_MIX, ["mk0t0", "mk0t1"], bT_hi, bT_lo, 0)
                down(NCH - 1, 0, LAST_DOWN if f == 1 else NU - 1, False, True)

            with pe.Fori(0, DEPTH) as l:
                ffn(l, 1, 0)

                def grp_scores(g):
                    for j in range(4):
                        pe.wait_ge(*room(l, f"s{g}_{j}"))
                    for b in range(2):
                        n = WIN * (b + 1)
                        for i in range(2):
                            for odd in range(2):
                                head, name = GRP * g + 2 * i + odd, f"s{g}_{2 * b + odd}"
                                rows = slice(HD * odd, HD * (odd + 1))
                                last = nc.tensor.matmul(bank(name)[:, i * n:(i + 1) * n], sqT[rows, head // 2, tokens(b)],
                                                        skT[rows, head // (SWA_H // SWA_KV), 0:n], start=True, stop=True)
                                if i == 1:
                                    last.then_inc(fullsem(name), 1)

                def grp_transposes(g):
                    pe.wait_ge(swa_exp, l * NGRP + (g + 1))
                    for j in range(3):
                        name = f"pt{g}_{j}"
                        pe.wait_ge(*room(l, name))
                        for i in range(4):
                            head, col = (i, 0) if j == 0 else (2 * (j - 1) + i // 2, WIN * (1 + i % 2))
                            last = nc.tensor.transpose(bank(name)[:, i * P:(i + 1) * P],
                                                       prob[:, g % 2, head, col:col + P], ident[:, :])
                        last.then_inc(fullsem(name), 1)

                def grp_values(g):
                    kv = GRP * g // (SWA_H // SWA_KV)
                    name = f"pv{g}_0"
                    wait_out(l, [f"pt{g}_{j}" for j in range(3)], [name])
                    pe.wait_ge(*room(l, name))
                    for i in range(GRP):
                        v = [sv[:, t, kv * HD:(kv + 1) * HD] for t in range(TT)]
                        o = bank(name)[:, 2 * i * HD:2 * (i + 1) * HD]
                        nc.tensor.matmul(o[:, 0:HD], pT[:, i, :], v[0], start=True, stop=True)
                        for t in range(TT):
                            last = nc.tensor.matmul(o[:, HD:2 * HD], pT[:, GRP + 2 * i + t, :], v[t],
                                                    start=t == 0, stop=t == TT - 1)
                    last.then_inc(fullsem(name), 1)

                def step(s):
                    if s in ("xt0", "xt1"):
                        h = int(s[2])
                        for t in range(TT):
                            pe.wait_ge(*out_of(l, f"down1_{h}{t}"))
                        x_transposes(l, s, h)
                    elif s == "yt0":
                        for t in range(TT):
                            pe.wait_ge(*out_of(l, f"wo0t{t}"))
                        x_transposes(l, "y0", 0)
                    elif s == "sqt":
                        wait_out(l, [f"sq{h}t{t}" for h in range(2) for t in range(TT)], ["sqt_0"])
                        for j in range(4):
                            transpose_to(l, f"sqt_{j}", token_major(stB), 2 * j)
                    elif s == "skt":
                        wait_out(l, [f"skvt{t}" for t in range(TT)], ["skt_0"])
                        transpose_to(l, "skt_0", lambda t, g: skd[:, t, g].rearrange("p a b -> p (a b)"), 0)
                    elif s == "mkt":
                        wait_out(l, [f"mk{h}t{t}" for h in range(2) for t in range(TT)], ["mkt_0"])
                        for j in range(4):
                            transpose_to(l, f"mkt_{j}", token_major(stA), 2 * j)
                    elif s in ("s0", "s1", "s2", "s3"):
                        grp_scores(int(s[1]))
                    elif s[:2] == "pt":
                        grp_transposes(int(s[2]))
                    elif s in ("pv0", "pv1", "pv2", "pv3"):
                        grp_values(int(s[2]))
                    elif s == "st":
                        wait_out(l, [f"pv{g}_0" for g in range(NGRP)], ["st_0"])
                        for j in range(4):
                            transpose_to(l, f"st_{j}", token_major(stA), 2 * j)
                    elif s in ("rqt", "rkt"):
                        qk = int(s == "rkt")
                        pe.wait_ge(rotated, l * 4 + 2 * (qk + 1))
                        for j in range(2):
                            transpose_to(l, f"{s}_{j}", lambda t, h: stB[:, t, (RET_H * qk + h) * P:(RET_H * qk + h + 1) * P],
                                         2 * j)
                    elif s == "rs":
                        wait_out(l, [f"{a}_{j}" for a in ("rqt", "rkt") for j in range(2)], ["rs_0"])
                        for h in range(RET_H):
                            name = f"rs_{h}"
                            pe.wait_ge(*room(l, name))
                            nc.tensor.matmul(bank(name)[:, 0:2 * P], rkT[:, h, 0:P], rqT[:, h, :], start=True, stop=True)
                            nc.tensor.matmul(bank(name)[:, 2 * P:3 * P], rkT[:, h, P:2 * P], rqT[:, h, P:2 * P],
                                             start=True, stop=True).then_inc(fullsem(name), 1)
                    elif s == "ro":
                        for h in range(RET_H):
                            name = f"ro_{h}"
                            wait_out(l, [f"rs_{h}"], [name])
                            pe.wait_ge(*room(l, name))
                            v = [rv[:, t, h * RET_DV:(h + 1) * RET_DV] for t in range(TT)]
                            nc.tensor.matmul(bank(name)[:, 0:RET_DV], sdec[:, h, 0:P], v[0], start=True, stop=True)
                            nc.tensor.matmul(bank(name)[:, RET_DV:], sdec[:, h, P:2 * P], v[0], start=True, stop=False)
                            nc.tensor.matmul(bank(name)[:, RET_DV:], sdec[:, h, 2 * P:3 * P], v[1],
                                             start=False, stop=True).then_inc(fullsem(name), 1)
                    elif s == "rt":
                        wait_out(l, [f"ro_{h}" for h in range(RET_H)], ["rt_0"])
                        for j in range(4):
                            transpose_to(l, f"rt_{j}", token_major(stB), 2 * j)
                    elif s == "mqt":
                        wait_out(l, [f"mq{h}t{t}" for h in range(2) for t in range(TT)], ["mqt_0"])
                        for j in range(4):
                            transpose_to(l, f"mqt_{j}", token_major(stA), 2 * j)
                    elif s == "ms":
                        wait_out(l, [f"mqt_{j}" for j in range(4)], ["ms_0"])
                        for h in range(MEM_H):
                            name = f"ms_{h}"
                            pe.wait_ge(*room(l, name))
                            for t in range(TT):
                                for k in range(2):
                                    last = nc.tensor.matmul(bank(name)[:, t * MEM:(t + 1) * MEM],
                                                            mqT[:, 2 * h + k, tokens(t)], mkT[:, 2 * h + k, :],
                                                            start=k == 0, stop=k == 1)
                            last.then_inc(fullsem(name), 1)
                    elif s == "mpt":
                        for h in range(MEM_H):
                            name = f"mpt_{h}"
                            pe.wait_ge(mem_probs, l * MEM_H + (h + 1))
                            transpose_to(l, name, lambda t, m: mprob[:, h, t, m * P:(m + 1) * P], 0)
                    elif s == "mpv":
                        for h in range(MEM_H):
                            name = f"mpv_{h}"
                            wait_out(l, [f"mpt_{h}"], [name])
                            pe.wait_ge(*room(l, name))
                            for j in range(2):
                                k = 2 * h + j
                                for m in range(2):
                                    last = nc.tensor.matmul(bank(name)[:, j * SEQ:(j + 1) * SEQ],
                                                            mv[:, m, k * P:(k + 1) * P], mpT[:, h, m, :],
                                                            start=m == 0, stop=m == 1)
                            last.then_inc(fullsem(name), 1)
                    elif s in ("mg0", "mg1"):
                        h = int(s[2])
                        pe.wait_ge(gates_used, l * 8 + (4 + TT * (h + 1)))
                        for j in range(2):
                            transpose_to(l, f"{s}_{j}", token_major(merged), UB * h + 2 * j)

                for s in STEPS:
                    if s[0] == "step":
                        step(s[1])
                        continue
                    _, i, chunk, half, _, inside = s
                    names = [f"{chunk}t{t}" for t in range(TT)]
                    if chunk == "skv":
                        project_kv(l, MIX_AT + i, names)
                        continue
                    hi, lo = (bT_hi, bT_lo) if chunk[0] == "u" or chunk[:2] in ("mk", "mv") else (hT_hi, hT_lo)
                    if i == 0:
                        continue
                    need = {("sq0", 0): ["xt0"], ("sq0", 1): ["xt1"], ("wo0", 0): ["mg0"], ("wo0", 1): ["mg1"]}
                    for name in need.get((chunk, half), []):
                        for j in range(2):
                            pe.wait_ge(*out_of(l, f"{name}_{j}"))
                    need = {"us0": "st", "ur0": "rt", "um0": "mpv"}
                    if chunk in need:
                        for j in range(2 * half, 2 * half + 2):
                            pe.wait_ge(*out_of(l, f"{need[chunk]}_{j}"))
                    project(l, MIX_AT + i, names, hi, lo, half, inside=(lambda: [step(n) for n in inside]) if inside else None)
                ffn(l, 2, FFN2_AT)

        @block.scalar
        def _(act):
            for dst, src in ((gains, gains_in), (ident, ident_in)):
                act.dma_start(dst[:], src).then_inc(consts_loaded, 16)

            def squares(src, dst, done):
                for t in range(TT):
                    nc.scalar.activation(junk[:, t, :], src[:, t, :], ACT.Square, scale=D ** -0.5, accum_out=dst[:, t:t + 1]).then_inc(done, 1)

            def split(l, unit, uc=0):
                s = unit % RING
                act.wait_ge(raw_loaded[s], l * (NU // RING * 16) + uc * 16 + (unit // RING + 1) * 16)
                before = unit - RING
                if before >= 0:
                    act.wait_ge(*used(l, before, uc))
                nc.scalar.activation(w_hi[:, s], raw[:, s], ACT.Copy).then_inc(hi_split, 1)

            def hi_parts(l, name, dst, k0, gain, c=0):
                act.wait_ge(*full(l, name, c))
                if gain is None:
                    nc.scalar.activation(dst[:, k0:k0 + 2, :].rearrange("p k t -> p (k t)"), bank(name)[:, :],
                                         ACT.Copy).then_inc(hisem(name), 1)
                    return
                for j in range(2):
                    k = k0 + j
                    i = nc.scalar.activation(dst[:, k, :], bank(name)[:, j * SEQ:(j + 1) * SEQ], ACT.Copy,
                                             scale=cur[:, gain + k:gain + k + 1])
                i.then_inc(hisem(name), 1)

            def ffn(l, f, at, gain):
                if f == 1:
                    for j in range(2):
                        hi_parts(l, f"x0_{j}", hT_hi, 2 * j, gain)
                    split(l, 1)
                for j in range(2):
                    hi_parts(l, "xy"[f - 1] + f"1_{j}", hT_hi, UB + 2 * j, gain)
                if f == 1:
                    split(l, 2)
                act_x_squares(l, 0 if f == 1 else 2)
                split(l, at + 3)
                act.wait_ge(rstd_ready, l * 3 + (1 if f == 1 else 3))

                def silu(c, first=False):
                    for t in range(TT):
                        up = f"up{f}_0t{t}" if first else f"up{f}t{t}"
                        act.wait_ge(*(full(l, up) if first else full(l, up, c - 1)))
                        nc.scalar.activation(act_s[:, t, :], bank(up)[:, 0:FC], ACT.Silu,
                                             scale=rstd[:, t:t + 1]).then_inc(silu_ready[t], 1)

                def turn(start, i):
                    hi_parts(l, f"gt{f}", gT_hi, 0, None, i + start)
                    split(l, at + 5 + 3 * start, i)
                    silu(i + (start + 1))
                    split(l, at + 6 + 3 * start, i)
                    split(l, at + 7 + 3 * start, i)

                silu(0, True)
                split(l, at + 4)
                if f == 1:
                    act.dma_start(memT[:, :, :], memt_in).then_inc(memt_loaded, 16)
                    act.dma_start(stB[:, :, :], mem_in.rearrange("(t p) d -> p t d", p=P)).then_inc(mem_loaded, 16)
                turn(0, 0)
                if f == 1:
                    act.wait_ge(memt_loaded, l * 16 + 16)
                    for k in range(KT):
                        i = nc.scalar.activation(bT_hi[:, k, :], memT[:, k, :], ACT.Copy,
                                                 scale=cur[:, G_MEM + k:G_MEM + k + 1])
                    i.then_inc(memt_hi, 1)
                    act.wait_ge(mem_loaded, l * 16 + 16)
                    squares(stB, msq_mem, mem_msq_ready)
                with act.Fori(0, NCH - 3) as i:
                    turn(1, i)
                c = NCH - 2
                hi_parts(l, f"gt{f}", gT_hi, 0, None, c)
                split(l, at + 5 + 3 * c)
                silu(c + 1)
                if f == 1:
                    split(l, at + 6 + 3 * c)
                else:
                    with act.If(l < DEPTH - 1):
                        split(l, NU)
                hi_parts(l, f"gt{f}", gT_hi, 0, None, c + 1)
                if f == 1:
                    for u in (7, 8, 9):
                        split(l, at + u + 3 * c)

            def act_x_squares(l, which):
                if which == 0:
                    for h in range(2):
                        act.wait_ge(x_loaded[h], 16)
                    for b in range(4):
                        x_of_layer_before(act, l, b)
                for h in range(2):
                    for t in range(TT):
                        if which:
                            act.wait_ge(*out_of(l, f"down1_{h}{t}" if which == 1 else f"wo{h}t{t}"))
                squares(x, msq, msq_ready)

            split(0, 0)

            act.wait_ge(consts_loaded, 16 * 2)
            with act.Fori(0, DEPTH) as l:
                nc.scalar.activation(cur[:, :], gains[:, bass.ds(l, 1), :].rearrange("p a g -> p (a g)"), ACT.Copy)\
                    .then_inc(layer_consts, 1)
                act.wait_ge(layer_consts, l + 1)
                ffn(l, 1, 0, G_FFN1)

                def scaled(dst, chunk, t, scale, func=ACT.Copy, cols=(0, BLK)):
                    name = f"{chunk}t{t}"
                    return nc.scalar.activation(dst, bank(name)[:, cols[0]:cols[1]], func, scale=scale[:, t:t + 1])

                def evacuate(chunk):
                    kind, half = chunk[:2], int(chunk[2]) if chunk != "skv" else 0
                    cols = slice(half * BLK, (half + 1) * BLK)
                    to = {"mk": stA, "mv": mv, "sq": stB, "rv": rv, "mq": stA, "rg": srg,
                          "gs": gates, "gr": gates, "gm": gates, "rq": stB, "rk": stB}
                    if kind in ("us", "ur", "um", "wo"):
                        return
                    if chunk == "mk0":
                        act.wait_ge(rstd_mem_ready, l + 1)
                        act.wait_ge(memt_lo, l + 1)
                    if chunk == "sq0":
                        act.wait_ge(rstd_ready, l * 3 + 2)
                    if kind == "rk":
                        cols = slice(BLK, 2 * BLK)
                    for t in range(TT):
                        name = f"{chunk}t{t}"
                        act.wait_ge(*full(l, name))
                        if kind == "gr":
                            act.wait_ge(*out_of(l, f"us{half}t{t}"))
                        if kind == "gm":
                            act.wait_ge(gates_used, l * 8 + (TT * half + t + 1))
                        if kind == "sk":
                            k = bank(name)[:, 0:SWA_KV * HD].rearrange("p (g d) -> p g d", g=SWA_KV)
                            for dup in range(2):
                                nc.scalar.activation(skd[:, t, :, dup, :], k, ACT.Copy, scale=rstd[:, t:t + 1])
                            scaled(sv[:, t, :], chunk, t, rstd, cols=(P, 2 * P)).then_inc(free(name), 1)
                        else:
                            func = ACT.Silu if kind == "rg" else ACT.Sigmoid if kind[0] == "g" else ACT.Copy
                            scaled(to[kind][:, t, cols], chunk, t, rstd_mem if kind in ("mk", "mv") else rstd,
                                   func).then_inc(free(name), 1)

                def copy_out(name, dst):
                    act.wait_ge(*full(l, name))
                    nc.scalar.activation(dst, bank(name)[:, :], ACT.Copy).then_inc(free(name), 1)

                def two(buf, j):
                    return buf[:, 2 * j:2 * j + 2, :].rearrange("p k t -> p (k t)")

                def step(s):
                    if s in ("xt0", "xt1"):
                        for j in range(2):
                            hi_parts(l, f"{s}_{j}", hT_hi, UB * int(s[2]) + 2 * j, G_MIX)
                        if s == "xt1":
                            act_x_squares(l, 1)
                    elif s == "yt0":
                        for j in range(2):
                            hi_parts(l, f"y0_{j}", hT_hi, 2 * j, G_FFN2)
                    elif s in ("mg0", "mg1"):
                        for j in range(2):
                            hi_parts(l, f"{s}_{j}", hT_hi, UB * int(s[2]) + 2 * j, None)
                    elif s in SPLIT_TO:
                        gain, hi, _ = SPLIT_TO[s]
                        for j in range(4):
                            hi_parts(l, f"{s}_{j}", hi, 2 * j, gain)
                    elif s == "sqt":
                        for j in range(4):
                            copy_out(f"sqt_{j}", two(sqT, j))
                    elif s == "skt":
                        copy_out("skt_0", skT[:, :, :].rearrange("p g t -> p (g t)"))
                    elif s == "mkt":
                        for j in range(4):
                            copy_out(f"mkt_{j}", two(mkT, j))
                    elif s == "mqt":
                        for j in range(4):
                            copy_out(f"mqt_{j}", two(mqT, j))
                    elif s == "rqt":
                        for j in range(2):
                            copy_out(f"rqt_{j}", two(rqT, j))
                    elif s == "rkt":
                        act.wait_ge(rotated, l * 4 + 4)
                        for j in range(2):
                            copy_out(f"rkt_{j}", two(rkT, j))
                    elif s[0] == "e":
                        g = int(s[1])
                        act.wait_ge(swa_max, l * NGRP + (g + 1))
                        nc.scalar.activation(sexp[:, g % 2], ssink[:, g % 2], ACT.Exp)
                        for i in range(GRP):
                            for b in range(2):
                                p = prob[:, g % 2, i, (0 if b == 0 else WIN):(WIN if b == 0 else 3 * WIN)]
                                last = nc.scalar.activation(p, p, ACT.Exp, bias=snm[:, g % 2, i, b:b + 1],
                                                            accum_out=ssum[:, g % 2, i, b:b + 1])
                        last.then_inc(swa_exp, 1)
                    elif s in ("pt0", "pt1", "pt2", "pt3"):
                        for j in range(3):
                            copy_out(f"{s}_{j}", pT[:, 4 * j:4 * j + 4, :].rearrange("p a b -> p (a b)"))
                    elif s == "ro":
                        for h in range(RET_H):
                            act.wait_ge(*full(l, f"ro_{h}"))
                            for t in range(TT):
                                nc.scalar.activation(junk[:, t, h * RET_DV:(h + 1) * RET_DV], bank(f"ro_{h}")[:, t * RET_DV:(t + 1) * RET_DV],
                                                     ACT.Square, scale=RET_DV ** -0.5, accum_out=msq_r[:, 2 * h + t:2 * h + t + 1])\
                                    .then_inc(retsq_ready, 1)
                    elif s == "me":
                        for h in range(MEM_H):
                            act.wait_ge(mem_max, l * MEM_H + (h + 1))
                            for t in range(TT):
                                last = nc.scalar.activation(mprob[:, h, t, :], bank(f"ms_{h}")[:, t * MEM:(t + 1) * MEM],
                                                            ACT.Exp, bias=mnm[:, h, t:t + 1], scale=MEM_HD ** -0.5,
                                                            accum_out=msum[:, h, t:t + 1])
                            last.then_inc(free(f"ms_{h}"), 1)
                    elif s == "mpt":
                        for h in range(MEM_H):
                            copy_out(f"mpt_{h}", mpT[:, h, :, :].rearrange("p m t -> p (m t)"))

                for s in STEPS:
                    if s[0] == "step":
                        step(s[1])
                        continue
                    _, i, chunk, _, last, inside = s
                    if i == 0:
                        continue
                    for name in inside:
                        step(name)
                    if last:
                        evacuate(chunk)
                    split(l, MIX_AT + i + RING)
                ffn(l, 2, FFN2_AT, G_FFN2)
            act.dma_start(gfin[:, :], gfin_in).then_inc(gfin_loaded, 16)
            for h in range(2):
                for t in range(TT):
                    x_of_layer_before(act, DEPTH, 2 * h + t)
                    cols = slice(h * BLK, (h + 1) * BLK)
                    nc.scalar.activation(junk[:, t, cols], x[:, t, cols], ACT.Square, scale=D ** -0.5,
                                         accum_out=msq_end[:, h, t:t + 1]).then_inc(end_msq, 1)

        @block.vector
        def _(dve):
            n = [0]

            def split(l, unit, uc=0):
                s = unit % RING
                dve.wait_ge(hi_split, l * NU + uc * RING + (unit + 1))
                nc.vector.tensor_tensor(w_lo[:, s], raw[:, s], w_hi[:, s].bitcast(F32), ALU.subtract).then_inc(lo_split, 1)

            def lo_parts(l, name, hi, lo, k0, gain, c=0):
                dve.wait_ge(*hi_out(l, name, c))
                if gain is None:
                    nc.vector.tensor_tensor(lo[:, k0:k0 + 2, :].rearrange("p k t -> p (k t)"), bank(name)[:, :],
                                            hi[:, k0:k0 + 2, :].bitcast(F32).rearrange("p k t -> p (k t)"),
                                            ALU.subtract).then_inc(free(name), 1)
                    return
                for j in range(2):
                    k = k0 + j
                    i = nc.vector.scalar_tensor_tensor(lo[:, k, :], bank(name)[:, j * SEQ:(j + 1) * SEQ],
                                                       cur[:, gain + k:gain + k + 1], hi[:, k, :].bitcast(F32),
                                                       op0=ALU.mult, op1=ALU.subtract)
                i.then_inc(free(name), 1)

            def ffn(l, f, at, gain):
                if f == 1:
                    for j in range(2):
                        lo_parts(l, f"x0_{j}", hT_hi, hT_lo, 2 * j, gain)
                    split(l, 1)
                for j in range(2):
                    lo_parts(l, "xy"[f - 1] + f"1_{j}", hT_hi, hT_lo, UB + 2 * j, gain)
                if f == 1:
                    split(l, 2)
                split(l, at + 3)
                dve.wait_ge(rstd_ready, l * 3 + (1 if f == 1 else 3))

                def times(c, first=False):
                    for t in range(TT):
                        up = f"up{f}_0t{t}" if first else f"up{f}t{t}"
                        dve.wait_ge(silu_ready[t], l * 2 * NCH + c + ((f - 1) * NCH + 1))
                        nc.vector.scalar_tensor_tensor(act_g[:, t, :], bank(up)[:, FC:2 * FC], rstd[:, t:t + 1],
                                                       act_s[:, t, :], op0=ALU.mult, op1=ALU.mult).then_inc(free(up), 1)

                def turn(start, i):
                    lo_parts(l, f"gt{f}", gT_hi, gT_lo, 0, None, i + start)
                    split(l, at + 5 + 3 * start, i)
                    times(i + (start + 1))
                    split(l, at + 6 + 3 * start, i)
                    split(l, at + 7 + 3 * start, i)

                times(0, True)
                split(l, at + 4)
                turn(0, 0)
                if f == 1:
                    dve.wait_ge(memt_hi, l + 1)
                    for k in range(KT):
                        i = nc.vector.scalar_tensor_tensor(bT_lo[:, k, :], memT[:, k, :],
                                                           cur[:, G_MEM + k:G_MEM + k + 1], bT_hi[:, k, :].bitcast(F32),
                                                           op0=ALU.mult, op1=ALU.subtract)
                    i.then_inc(memt_lo, 1)
                with dve.Fori(0, NCH - 3) as i:
                    turn(1, i)
                c = NCH - 2
                lo_parts(l, f"gt{f}", gT_hi, gT_lo, 0, None, c)
                split(l, at + 5 + 3 * c)
                times(c + 1)
                if f == 1:
                    split(l, at + 6 + 3 * c)
                else:
                    with dve.If(l < DEPTH - 1):
                        split(l, NU)
                lo_parts(l, f"gt{f}", gT_hi, gT_lo, 0, None, c + 1)
                if f == 1:
                    for u in (7, 8):
                        split(l, at + u + 3 * c)
                for h in range(2):
                    for t in range(TT):
                        nm = f"down{f}_{h}{t}"
                        dve.wait_ge(*full(l, nm))
                        xs = x[:, t, h * BLK:(h + 1) * BLK]
                        nc.vector.scalar_tensor_tensor(xs, bank(nm)[:, :], 0.5, xs, op0=ALU.mult, op1=ALU.add)\
                            .then_inc(free(nm), 1)
                if f == 1:
                    split(l, at + 9 + 3 * c)

            dve.wait_ge(consts_loaded, 16 * 2)
            split(0, 0)
            with dve.Fori(0, DEPTH) as l:
                n[0] = 0

                def own(i):
                    n[0] += 1
                    return i.then_inc(dve_step, 1)

                def settled():
                    dve.wait_ge(dve_step, l * DVE_STEPS + n[0])

                dve.wait_ge(layer_consts, l + 1)
                ffn(l, 1, 0, G_FFN1)

                dve.wait_ge(tables_loaded, 16 * 3)

                def evacuate(chunk):
                    kind, half = chunk[:2], chunk[2]
                    if kind not in ("us", "ur", "um", "wo"):
                        return
                    half = int(half)
                    for t in range(TT):
                        name = f"{chunk}t{t}"
                        dve.wait_ge(*full(l, name))
                        cols = slice(half * BLK, (half + 1) * BLK)
                        g, m = gates[:, t, cols], merged[:, t, cols]
                        if kind == "wo":
                            xs = x[:, t, cols]
                            nc.vector.tensor_tensor(xs, bank(name)[:, :], xs, ALU.add)\
                                .then_inc(free(name), 1)
                            continue
                        gate = {"us": "gs", "ur": "gr", "um": "gm"}[kind] + f"{half}t{t}"
                        dve.wait_ge(*out_of(l, gate))
                        if kind == "us":
                            nc.vector.tensor_tensor(m, bank(name)[:, :], g, ALU.mult).then_inc(free(name), 1)
                        else:
                            nc.vector.tensor_tensor(g, bank(name)[:, :], g, ALU.mult).then_inc(free(name), 1)
                            dve.wait_ge(*out_of(l, name))
                            nc.vector.tensor_tensor(m, m, g, ALU.add).then_inc(gates_used, 1)

                def step(s):
                    if s in ("xt0", "xt1"):
                        for j in range(2):
                            lo_parts(l, f"{s}_{j}", hT_hi, hT_lo, UB * int(s[2]) + 2 * j, G_MIX)
                    elif s == "yt0":
                        for j in range(2):
                            lo_parts(l, f"y0_{j}", hT_hi, hT_lo, 2 * j, G_FFN2)
                    elif s in ("mg0", "mg1"):
                        for j in range(2):
                            lo_parts(l, f"{s}_{j}", hT_hi, hT_lo, UB * int(s[2]) + 2 * j, None)
                    elif s in SPLIT_TO:
                        gain, hi, lo = SPLIT_TO[s]
                        for j in range(4):
                            lo_parts(l, f"{s}_{j}", hi, lo, 2 * j, gain)
                    elif s in ("s0", "s1", "s2", "s3"):
                        g = int(s[1])
                        pr, par = prob[:, g % 2], g % 2
                        for j in range(4):
                            name, (b, odd) = f"s{g}_{j}", divmod(j, 2)
                            w = WIN * (b + 1)
                            src = bank(name)[:, 0:2 * w].rearrange("p (h k) -> p h k", h=2)
                            dst = pr[:, odd::2, 0:WIN] if b == 0 else pr[:, odd::2, WIN:3 * WIN]
                            msk = (mask[:, WIN:] if b == 0 else mask[:, :]).unsqueeze(1).broadcast_to([P, 2, w])
                            dve.wait_ge(*full(l, name))
                            nc.vector.scalar_tensor_tensor(dst, src, HD ** -0.5, msk, op0=ALU.mult, op1=ALU.add)\
                                .then_inc(free(name), 1)
                        for j in range(4):
                            dve.wait_ge(*out_of(l, f"s{g}_{j}"))
                        nc.vector.tensor_reduce(smax[:, par, :, 0], pr[:, :, 0:WIN], axis=AXX, op=ALU.max)
                        own(nc.vector.tensor_reduce(smax[:, par, :, 1], pr[:, :, WIN:3 * WIN], axis=AXX, op=ALU.max))
                        settled()
                        sink = cur[:, G_SINK + GRP * g:G_SINK + GRP * (g + 1)].unsqueeze(2).broadcast_to([P, GRP, 2])
                        own(nc.vector.tensor_tensor(smax[:, par], smax[:, par], sink, ALU.max))
                        settled()
                        nc.vector.tensor_scalar(snm[:, par], smax[:, par], -1.0, None, ALU.mult)
                        nc.vector.tensor_tensor(ssink[:, par], sink, smax[:, par], ALU.subtract).then_inc(swa_max, 1)
                    elif s in ("pv0", "pv1", "pv2", "pv3"):
                        g = int(s[2])
                        par = g % 2
                        dve.wait_ge(swa_exp, l * NGRP + (g + 1))
                        own(nc.vector.tensor_tensor(ssum[:, par], ssum[:, par], sexp[:, par], ALU.add))
                        settled()
                        own(nc.vector.reciprocal(ssum[:, par], ssum[:, par]))
                        settled()
                        name = f"pv{g}_0"
                        dve.wait_ge(*full(l, name))
                        for t in range(TT):
                            o = bank(name)[:, :].rearrange("p (h b d) -> p h b d", h=GRP, b=2)[:, :, t, :]
                            dst = stA[:, t, GRP * HD * g:GRP * HD * (g + 1)].rearrange("p (h d) -> p h d", h=GRP)
                            i = nc.vector.tensor_tensor(dst, o, ssum[:, par, :, t:t + 1].broadcast_to([P, GRP, HD]), ALU.mult)
                        i.then_inc(free(name), 1)
                    elif s == "rs":
                        for h in range(RET_H):
                            name = f"rs_{h}"
                            dve.wait_ge(*full(l, name))
                            nc.vector.tensor_tensor(sdec[:, h, 0:2 * P], bank(name)[:, 0:2 * P], decay[:, h, :], ALU.mult)
                            nc.vector.tensor_tensor(sdec[:, h, 2 * P:], bank(name)[:, 2 * P:3 * P], decay[:, h, 0:P],
                                                    ALU.mult).then_inc(free(name), 1)
                    elif s == "re":
                        dve.wait_ge(retstd_ready, l + 1)
                        for t in range(TT):
                            dve.wait_ge(*out_of(l, f"rg1t{t}"))
                        for h in range(RET_H):
                            name = f"ro_{h}"
                            for t in range(TT):
                                cols = slice(h * RET_DV, (h + 1) * RET_DV)
                                i = nc.vector.scalar_tensor_tensor(stB[:, t, cols], bank(name)[:, t * RET_DV:(t + 1) * RET_DV],
                                                                   rstd_r[:, 2 * h + t:2 * h + t + 1], srg[:, t, cols],
                                                                   op0=ALU.mult, op1=ALU.mult)
                            i.then_inc(free(name), 1)
                    elif s == "ms":
                        for h in range(MEM_H):
                            name = f"ms_{h}"
                            dve.wait_ge(*full(l, name))
                            own(nc.vector.tensor_reduce(mmax[:, h, :], bank(name)[:, :].rearrange("p (t m) -> p t m", t=TT),
                                                        axis=AXX, op=ALU.max))
                            settled()
                            nc.vector.tensor_scalar(mnm[:, h, :], mmax[:, h, :], -(MEM_HD ** -0.5), None, ALU.mult)\
                                .then_inc(mem_max, 1)
                    elif s == "mn":
                        for h in range(MEM_H):
                            dve.wait_ge(*out_of(l, f"ms_{h}"))
                            own(nc.vector.reciprocal(msum[:, h, :], msum[:, h, :]))
                            settled()
                            nc.vector.tensor_tensor(mprob[:, h], mprob[:, h],
                                                    msum[:, h, :].unsqueeze(2).broadcast_to([P, TT, MEM]), ALU.mult)\
                                .then_inc(mem_probs, 1)

                for s in STEPS:
                    if s[0] == "step":
                        step(s[1])
                        continue
                    _, i, chunk, _, last, inside = s
                    if i == 0:
                        continue
                    for name in inside:
                        step(name)
                    if last:
                        evacuate(chunk)
                    split(l, MIX_AT + i + RING)
                ffn(l, 2, FFN2_AT, G_FFN2)
                assert n[0] == DVE_STEPS, n
            dve.wait_ge(gfin_loaded, 16)
            for t in range(TT):
                dve.wait_ge(rstd_ready, DEPTH * 3 + (t + 1))
                for h in range(2):
                    cols = slice(h * BLK, (h + 1) * BLK)
                    nc.vector.scalar_tensor_tensor(stB[:, t, cols], x[:, t, cols], rstd[:, t:t + 1], gfin[:, cols],
                                                   op0=ALU.mult, op1=ALU.mult).then_inc(final_ready, 1)


def _ffn_units(w1, w3, w2):
    up = np.stack([w1.reshape(KT, P, NCH, FC), w3.reshape(KT, P, NCH, FC)], axis=3)
    up = up.transpose(2, 0, 1, 3, 4).reshape(NCH, 2, UB, P, BLK).transpose(0, 1, 3, 2, 4).reshape(NCH, 2, P, UW)
    down = w2.reshape(NCH, 2, P, 2, BLK).transpose(0, 2, 3, 1, 4).reshape(NCH, P, UW)
    units = list(up[0])
    for c in range(NCH - 1):
        units += [*up[c + 1], down[c]]
    return units + [down[NCH - 1]]


def _mix_units(w_in, w_kv, w_ur, w_us, w_um, w_o):
    units = []
    for c, u, _ in UNITS:
        kind, half = c[:2], c[2]
        if c == "skv":
            at = W_IN_AT["skv"]
            units.append(w_in[:, at:at + 256].reshape(KT, P, 256).transpose(1, 0, 2).reshape(P, UW))
            continue
        at = int(half) * BLK
        if kind in ("mk", "mv"):
            w, at = w_kv, at + (D if kind == "mv" else 0)
        elif kind in ("us", "ur", "um", "wo"):
            w = {"us": w_us, "ur": w_ur, "um": w_um, "wo": w_o}[kind]
        elif kind[0] == "g":
            w, at = w_in, W_IN_AT["gl"] + "rsm".index(kind[1]) * D + at
        else:
            w, at = w_in, W_IN_AT[kind] + at
        units.append(w[u * UB * P:(u + 1) * UB * P, at:at + BLK].reshape(UB, P, BLK).transpose(1, 0, 2).reshape(P, UW))
    return units


def _tables():
    f = np.float32
    half = RET_DK // 2
    inv = f(10000.0) ** (-np.arange(half, dtype=f) / f(half))
    ang = np.arange(SEQ, dtype=f)[:, None] * inv[None, :]
    cos, sin = np.cos(ang), np.sin(ang)
    rot = np.stack([np.concatenate([cos, cos], 1), np.concatenate([-sin, sin], 1)])
    rot = rot.reshape(2, TT, P, P).transpose(2, 0, 1, 3)
    log_g = np.log1p(-(f(2.0) ** (f(-5.0) - np.arange(RET_H, dtype=f)))).astype(f)
    i = np.arange(P, dtype=f)
    diff = i[None, :] - i[:, None]
    own = np.where(diff[None] >= 0, np.exp(np.maximum(diff, f(0))[None] * log_g[:, None, None]), f(0))
    cross = np.exp((diff[None] + f(P)) * log_g[:, None, None])
    decay = (np.concatenate([own, cross], 2) * f(RET_DK ** -0.5)).transpose(1, 0, 2)
    rel = np.arange(WIN)[:, None] + WIN - np.arange(2 * WIN)[None, :]
    mask = np.where((rel >= 0) & (rel < WIN), f(0), f(-1e30))
    return [np.ascontiguousarray(a.astype(f)) for a in (rot, decay, mask, np.eye(P, dtype=f))]


def kernel(x, mem, norm_ffn1, ffn1_w1, ffn1_w3, ffn1_w2, norm_mix, w_in, ret_gn, swa_sinks, norm_mem, w_mem_kv,
           w_up_ret, w_up_swa, w_up_mem, w_o, norm_ffn2, ffn2_w1, ffn2_w3, ffn2_w2, norm_final):
    import concourse.bacc as bacc
    from concourse.bass_utils import run_bass_kernel_spmd

    a = {k: np.asarray(v) for k, v in locals().items() if k not in ("bacc", "run_bass_kernel_spmd")}
    units = []
    for l in range(DEPTH):
        units += _ffn_units(a["ffn1_w1"][l], a["ffn1_w3"][l], a["ffn1_w2"][l])
        units += _mix_units(*(a[n][l] for n in ("w_in", "w_mem_kv", "w_up_ret", "w_up_swa", "w_up_mem", "w_o")))
        units[-MIX_UNITS - 1], units[-MIX_UNITS] = units[-MIX_UNITS], units[-MIX_UNITS - 1]
        units += _ffn_units(a["ffn2_w1"][l], a["ffn2_w3"][l], a["ffn2_w2"][l])
    gains = np.stack([np.concatenate(
        [a[n][l].reshape(KT, P).T for n in ("norm_ffn1", "norm_mix", "norm_mem", "ret_gn", "norm_ffn2")]
        + [np.broadcast_to(a["swa_sinks"][l], (P, SWA_H))], axis=1) for l in range(DEPTH)], axis=1)
    rot, decay, mask, ident = _tables()
    arrays = {
        "x": a["x"][0], "mem": a["mem"][0], "memt": a["mem"][0].T.reshape(KT, P, MEM).transpose(1, 0, 2),
        "stream": np.stack(units), "gains": gains, "gfin": np.broadcast_to(a["norm_final"], (P, D)),
        "rot": rot, "decay": decay, "mask": mask, "ident": ident,
    }
    nc = bacc.Bacc("TRN2", target_bir_lowering=False, num_devices=1)
    arrays = {f"in_{k}": np.ascontiguousarray(v) for k, v in arrays.items()}
    args = [nc.dram_tensor(k, v.shape, mybir.dt.from_np(v.dtype), kind="ExternalInput").ap() for k, v in arrays.items()]
    out = nc.dram_tensor("out", (SEQ, D), F32, kind="ExternalOutput").ap()
    build(nc, *args, out)
    got = run_bass_kernel_spmd(nc, [arrays], core_ids=[0]).results[0]["out"]
    return got.reshape(a["x"].shape)
```
